# Optimizing a Trainium2 kernel written in Bass

```python
import jax, jax.numpy as jnp
from jax import lax
import numpy as np
import jax
import jax.numpy as jnp

D_MODEL = 1024
BATCH = 1
SEQ = 256
DEPTH = 2

N_HEADS = 8
HEAD_DIM = 128
N_KV_HEADS = 2
ROPE_FRACTION_DIV = 4
ROPE_THETA = 500000.0
IDX_HEADS = 8
IDX_DIM = 64
TOPK_MAX = 256
Q_BLOCK = 128
CONF_WIDTH = D_MODEL
CONF_KERNEL = 31
SC_WIDTH = D_MODEL
SC_KERNEL = 3
FFN_DIM = 2816
FFN_KERNEL = 3
N_BRANCH = 3
NORM_EPS = 1e-6

Q_COLS = N_HEADS * HEAD_DIM
KV_COLS = N_KV_HEADS * HEAD_DIM
IQ_COLS = IDX_HEADS * IDX_DIM
IK_COLS = IDX_DIM
IW_COLS = IDX_HEADS
A_COLS = 2 * CONF_WIDTH
C_COLS = 3 * SC_WIDTH
G_COLS = N_BRANCH * D_MODEL
_IN_SIZES = (Q_COLS, KV_COLS, KV_COLS, IQ_COLS, IK_COLS, IW_COLS, A_COLS, C_COLS, G_COLS)
N_IN = sum(_IN_SIZES)
IN_SPLITS = tuple(sum(_IN_SIZES[:i + 1]) for i in range(len(_IN_SIZES) - 1))


def rms_norm(x, g):
    xf = x.astype(jnp.float32)
    r = lax.rsqrt(jnp.mean(xf * xf, axis=-1, keepdims=True) + NORM_EPS)
    return (xf * r * g.astype(jnp.float32)).astype(x.dtype)

def layer_norm(x, g, b):
    xf = x.astype(jnp.float32)
    mu = jnp.mean(xf, axis=-1, keepdims=True)
    xc = xf - mu
    r = lax.rsqrt(jnp.mean(xc * xc, axis=-1, keepdims=True) + NORM_EPS)
    return (xc * r * g.astype(jnp.float32) + b.astype(jnp.float32)).astype(x.dtype)

def causal_dwconv(x, w):
    K, C = w.shape
    return lax.conv_general_dilated(
        x, w[:, None, :].astype(x.dtype), window_strides=(1,), padding=[(K - 1, 0)],
        dimension_numbers=("NWC", "WIO", "NWC"), feature_group_count=C)

def rope_tables(seq_len, rot_dim):
    pos = jnp.arange(seq_len, dtype=jnp.float32)
    inv_freq = jnp.power(ROPE_THETA, -jnp.arange(0, rot_dim, 2, dtype=jnp.float32) / rot_dim)
    ang = pos[:, None] * inv_freq[None, :]
    return jnp.cos(ang), jnp.sin(ang)

def partial_rope(x, cos, sin):
    half = cos.shape[-1]
    xf = x.astype(jnp.float32)
    x1, x2, xp = xf[..., :half], xf[..., half:2 * half], xf[..., 2 * half:]
    c = cos[None, :, None, :]
    s = sin[None, :, None, :]
    out = jnp.concatenate([x1 * c - x2 * s, x2 * c + x1 * s, xp], axis=-1)
    return out.astype(x.dtype)

def dsa_attention(q, k, v, iq, ik, iw):
    B, S, H, dh = q.shape
    G = k.shape[2]
    rep = H // G
    k_sel = min(TOPK_MAX, S // 4)
    n_blocks = S // Q_BLOCK
    key_pos = jnp.arange(S)
    scale = HEAD_DIM ** -0.5
    gather = jax.vmap(lambda arr, idx: arr[idx])

    def block(i):
        t0 = i * Q_BLOCK
        qb = lax.dynamic_slice_in_dim(q, t0, Q_BLOCK, axis=1)
        iqb = lax.dynamic_slice_in_dim(iq, t0, Q_BLOCK, axis=1)
        iwb = lax.dynamic_slice_in_dim(iw, t0, Q_BLOCK, axis=1)
        q_pos = t0 + jnp.arange(Q_BLOCK)
        rel = jax.nn.relu(jnp.einsum('bthd,bsd->bths', iqb, ik).astype(jnp.float32))
        score = jnp.einsum('bths,bth->bts', rel, iwb.astype(jnp.float32))
        causal = key_pos[None, :] <= q_pos[:, None]
        score = jnp.where(causal[None], score, -jnp.inf)
        _, idx = lax.top_k(score, k_sel)
        valid = idx <= q_pos[None, :, None]
        flat = idx.reshape(B, Q_BLOCK * k_sel)
        kg = gather(k, flat).reshape(B, Q_BLOCK, k_sel, G, dh)
        vg = gather(v, flat).reshape(B, Q_BLOCK, k_sel, G, dh)
        qg = qb.reshape(B, Q_BLOCK, G, rep, dh)
        logits = jnp.einsum('btgrd,btkgd->btgrk', qg, kg).astype(jnp.float32) * scale
        logits = jnp.where(valid[:, :, None, None, :], logits, -jnp.inf)
        p = jax.nn.softmax(logits, axis=-1).astype(v.dtype)
        o = jnp.einsum('btgrk,btkgd->btgrd', p, vg)
        return o.reshape(B, Q_BLOCK, H * dh)

    out = lax.map(block, jnp.arange(n_blocks))
    return out.transpose(1, 0, 2, 3).reshape(B, S, H * dh)

def hybrid_layer(x, rope_attn, rope_idx, norm1_g, w_in, q_norm_g, k_norm_g, w_attn_out,
                 conf_conv_w, conf_conv_b, conf_ln_g, conf_ln_b, w_conf_out,
                 sc_conv_w, w_sc_out, w_o, norm2_g, w_up, ffn_conv_w, ffn_conv_b, w_down):
    B, S, _ = x.shape
    h = rms_norm(x, norm1_g)
    proj = h @ w_in
    q, k, v, iq, ik, iw, a_in, c_in, g_in = jnp.split(proj, IN_SPLITS, axis=-1)

    q = partial_rope(rms_norm(q.reshape(B, S, N_HEADS, HEAD_DIM), q_norm_g), *rope_attn)
    k = partial_rope(rms_norm(k.reshape(B, S, N_KV_HEADS, HEAD_DIM), k_norm_g), *rope_attn)
    v = v.reshape(B, S, N_KV_HEADS, HEAD_DIM)
    iq = partial_rope(iq.reshape(B, S, IDX_HEADS, IDX_DIM), *rope_idx)
    ik = partial_rope(ik[:, :, None, :], *rope_idx)[:, :, 0, :]
    iw = iw * (IDX_HEADS ** -0.5 * IDX_DIM ** -0.5)
    y_attn = dsa_attention(q, k, v, iq, ik, iw) @ w_attn_out

    a_val, a_gate = jnp.split(a_in, 2, axis=-1)
    a = causal_dwconv(a_val * jax.nn.sigmoid(a_gate), conf_conv_w) + conf_conv_b
    y_conf = jax.nn.silu(layer_norm(a, conf_ln_g, conf_ln_b)) @ w_conf_out

    c_b, c_c, c_x = jnp.split(c_in, 3, axis=-1)
    y_sc = (c_b * causal_dwconv(c_c * c_x, sc_conv_w)) @ w_sc_out

    gates = jax.nn.sigmoid(g_in.reshape(B, S, N_BRANCH, D_MODEL).astype(jnp.float32)).astype(x.dtype)
    merged = gates[:, :, 0] * y_conf + gates[:, :, 1] * y_attn + gates[:, :, 2] * y_sc
    x = x + merged @ w_o

    u = causal_dwconv(rms_norm(x, norm2_g) @ w_up, ffn_conv_w) + ffn_conv_b
    u_gate, u_val = jnp.split(u, 2, axis=-1)
    return x + (jax.nn.silu(u_gate) * u_val) @ w_down

def first_inputs(seed: int = 0) -> dict:
    key = jax.random.key(seed)
    ks = jax.random.split(key, 20)
    f32 = jnp.float32

    def nrm(k, shape, scale):
        return jax.random.normal(k, shape, f32) * scale

    L = DEPTH
    return {
        "x": nrm(ks[0], (BATCH, SEQ, D_MODEL), 1.0),
        "norm1_g": 1.0 + nrm(ks[1], (L, D_MODEL), 0.05),
        "w_in": nrm(ks[2], (L, D_MODEL, N_IN), D_MODEL ** -0.5),
        "q_norm_g": 1.0 + nrm(ks[3], (L, HEAD_DIM), 0.05),
        "k_norm_g": 1.0 + nrm(ks[4], (L, HEAD_DIM), 0.05),
        "w_attn_out": nrm(ks[5], (L, Q_COLS, D_MODEL), Q_COLS ** -0.5),
        "conf_conv_w": nrm(ks[6], (L, CONF_KERNEL, CONF_WIDTH), CONF_KERNEL ** -0.5),
        "conf_conv_b": nrm(ks[7], (L, CONF_WIDTH), 0.01),
        "conf_ln_g": 1.0 + nrm(ks[8], (L, CONF_WIDTH), 0.05),
        "conf_ln_b": nrm(ks[9], (L, CONF_WIDTH), 0.01),
        "w_conf_out": nrm(ks[10], (L, CONF_WIDTH, D_MODEL), CONF_WIDTH ** -0.5),
        "sc_conv_w": nrm(ks[11], (L, SC_KERNEL, SC_WIDTH), SC_KERNEL ** -0.5),
        "w_sc_out": nrm(ks[12], (L, SC_WIDTH, D_MODEL), SC_WIDTH ** -0.5),
        "w_o": nrm(ks[13], (L, D_MODEL, D_MODEL), D_MODEL ** -0.5),
        "norm2_g": 1.0 + nrm(ks[14], (L, D_MODEL), 0.05),
        "w_up": nrm(ks[15], (L, D_MODEL, 2 * FFN_DIM), D_MODEL ** -0.5),
        "ffn_conv_w": nrm(ks[16], (L, FFN_KERNEL, 2 * FFN_DIM), FFN_KERNEL ** -0.5),
        "ffn_conv_b": nrm(ks[17], (L, 2 * FFN_DIM), 0.01),
        "w_down": nrm(ks[18], (L, FFN_DIM, D_MODEL), FFN_DIM ** -0.5),
    }

def first_block(x, norm1_g, w_in, q_norm_g, k_norm_g, w_attn_out, conf_conv_w, conf_conv_b,
              conf_ln_g, conf_ln_b, w_conf_out, sc_conv_w, w_sc_out, w_o, norm2_g, w_up,
              ffn_conv_w, ffn_conv_b, w_down):
    S = x.shape[1]
    rope_attn = rope_tables(S, HEAD_DIM // ROPE_FRACTION_DIV)
    rope_idx = rope_tables(S, IDX_DIM // ROPE_FRACTION_DIV)
    for l in range(DEPTH):
        x = hybrid_layer(x, rope_attn, rope_idx, norm1_g[l], w_in[l], q_norm_g[l], k_norm_g[l],
                         w_attn_out[l], conf_conv_w[l], conf_conv_b[l], conf_ln_g[l], conf_ln_b[l],
                         w_conf_out[l], sc_conv_w[l], w_sc_out[l], w_o[l], norm2_g[l], w_up[l],
                         ffn_conv_w[l], ffn_conv_b[l], w_down[l])
    return x


CTX_LEN = 256
GRID_W = 64
HEAD_DIM_2 = D_MODEL // 16
N_FOURIER_GROUPS = 4
N_NA_HEADS = 4
N_GLA_HEADS = 4
N_GQA_HEADS = 4
N_GQA_KV_HEADS = 2
GQA_GROUP = N_GQA_HEADS // N_GQA_KV_HEADS
GLA_DK = HEAD_DIM_2 // 2
GLA_DV = HEAD_DIM_2
GLA_GATE_RANK = 16
GLA_TAU = 16.0
GLA_CHUNK = 64
NA_ROWS = 8
NA_COLS = 16
D_FF = 256 * ((8 * D_MODEL // 3 + 255) // 256)
ROPE_THETA_2 = 10000.0
EPS = 1e-6
N_MOD = 9

W_FOURIER = N_FOURIER_GROUPS * HEAD_DIM_2
W_NA = N_NA_HEADS * HEAD_DIM_2
W_GLA = N_GLA_HEADS * GLA_DV
W_GQA = N_GQA_HEADS * HEAD_DIM_2
D_MIX = W_FOURIER + W_NA + W_GLA + W_GQA

IN_LAYOUT = (
    ('fourier', W_FOURIER),
    ('na_q', W_NA), ('na_k', W_NA), ('na_v', W_NA),
    ('gla_q', N_GLA_HEADS * GLA_DK), ('gla_k', N_GLA_HEADS * GLA_DK),
    ('gla_v', W_GLA), ('gla_r', W_GLA),
    ('gla_gf', GLA_GATE_RANK), ('gla_gb', GLA_GATE_RANK),
    ('gqa_q', W_GQA), ('gqa_k', N_GQA_KV_HEADS * HEAD_DIM_2), ('gqa_v', N_GQA_KV_HEADS * HEAD_DIM_2),
)
D_IN = sum(w for _, w in IN_LAYOUT)


def rms_norm_2(x, gain=None):
    xf = x.astype(jnp.float32)
    y = xf * lax.rsqrt(jnp.mean(xf * xf, axis=-1, keepdims=True) + EPS)
    if gain is not None:
        y = y * gain.astype(jnp.float32)
    return y.astype(x.dtype)

def modulate(h, shift, scale):
    return h * (1.0 + scale) + shift

def swiglu(h, w1, w3, w2):
    return (jax.nn.silu(h @ w1) * (h @ w3)) @ w2

def heads(t, n, d):
    return t.reshape(t.shape[:-1] + (n, d))

def split_in(h):
    offsets = np.cumsum([w for _, w in IN_LAYOUT])[:-1].tolist()
    parts = jnp.split(h, offsets, axis=-1)
    return {name: part for (name, _), part in zip(IN_LAYOUT, parts)}

def axial_rope(n_tokens):
    t = jnp.arange(n_tokens, dtype=jnp.int32)
    row = (t // GRID_W).astype(jnp.float32)
    col = (t % GRID_W).astype(jnp.float32)
    n_freq = HEAD_DIM_2 // 4
    inv_freq = ROPE_THETA_2 ** (-jnp.arange(n_freq, dtype=jnp.float32) / n_freq)
    ang = jnp.concatenate([row[:, None] * inv_freq, col[:, None] * inv_freq], axis=-1)
    return jnp.cos(ang)[:, None, :], jnp.sin(ang)[:, None, :]

def apply_rope(x, cos, sin):
    xf = x.astype(jnp.float32)
    x1, x2 = jnp.split(xf, 2, axis=-1)
    return jnp.concatenate([x1 * cos - x2 * sin, x1 * sin + x2 * cos], axis=-1).astype(x.dtype)

def fourier_mix(u):
    b_, l_, _ = u.shape
    uf = u.astype(jnp.float32).reshape(b_, l_, N_FOURIER_GROUPS, HEAD_DIM_2)
    y = jnp.fft.fft2(uf, axes=(1, 3), norm='ortho').real
    return y.reshape(b_, l_, W_FOURIER).astype(u.dtype)

def block_attention(q, k, v):
    b_, lq, hk, g, dh = q.shape
    nb = lq // Q_BLOCK
    qb = (q * dh ** -0.5).reshape(b_, nb, Q_BLOCK, hk, g, dh).swapaxes(0, 1)

    def one_block(q_blk):
        s = jnp.einsum('bqhgd,bkhd->bhgqk', q_blk, k).astype(jnp.float32)
        p = jax.nn.softmax(s, axis=-1).astype(v.dtype)
        return jnp.einsum('bhgqk,bkhd->bqhgd', p, v)

    o = lax.map(one_block, qb)
    return o.swapaxes(0, 1).reshape(b_, lq, hk * g * dh)

def neighborhood_attention(q, k, v, k_ctx, v_ctx, rpb):
    b_, s_, h_, dh = q.shape
    rows = s_ // GRID_W
    kr = min(NA_ROWS, rows)
    kg = k.reshape(b_, rows, GRID_W, h_, dh)
    vg = v.reshape(b_, rows, GRID_W, h_, dh)
    qg = q.reshape(b_, rows, GRID_W, h_, dh).transpose(1, 0, 2, 3, 4)
    r_pos = jnp.arange(rows)
    c_pos = jnp.arange(GRID_W)
    row_start = jnp.clip(r_pos - kr // 2, 0, rows - kr)
    rel_row = row_start[:, None] + jnp.arange(kr)[None, :] - r_pos[:, None]
    col_start = jnp.clip(c_pos - NA_COLS // 2, 0, GRID_W - NA_COLS)
    col_idx = col_start[:, None] + jnp.arange(NA_COLS)[None, :]
    rel_col = col_idx - c_pos[:, None]
    bias_col = rpb.astype(jnp.float32)[:, :, rel_col + NA_COLS - 1]
    scale = dh ** -0.5
    n_win = kr * NA_COLS

    def row_block(args):
        q_r, rs, rr = args
        k_blk = lax.dynamic_slice_in_dim(kg, rs, kr, axis=1)[:, :, col_idx]
        v_blk = lax.dynamic_slice_in_dim(vg, rs, kr, axis=1)[:, :, col_idx]
        bias = bias_col[:, rr + NA_ROWS - 1].transpose(0, 2, 1, 3)
        s_win = jnp.einsum('bchd,brckhd->bhcrk', q_r, k_blk).astype(jnp.float32) * scale + bias[None]
        s_ctx = jnp.einsum('bchd,bjhd->bhcj', q_r, k_ctx).astype(jnp.float32) * scale
        s = jnp.concatenate([s_win.reshape(b_, h_, GRID_W, n_win), s_ctx], axis=-1)
        p = jax.nn.softmax(s, axis=-1).astype(v.dtype)
        p_win = p[..., :n_win].reshape(b_, h_, GRID_W, kr, NA_COLS)
        p_ctx = p[..., n_win:]
        return (jnp.einsum('bhcrk,brckhd->bchd', p_win, v_blk)
                + jnp.einsum('bhcj,bjhd->bchd', p_ctx, v_ctx))

    out = lax.map(row_block, (qg, row_start, rel_row))
    return out.transpose(1, 0, 2, 3, 4).reshape(b_, s_, h_ * dh)

def gla_scan(q, k, v, log_a, s0):
    b_, h_, l_, _ = q.shape
    dv = v.shape[-1]
    n_chunks = l_ // GLA_CHUNK

    def chunks(t):
        return t.reshape(b_, h_, n_chunks, GLA_CHUNK, t.shape[-1]).transpose(2, 0, 1, 3, 4)

    lower_tri = jnp.tril(jnp.ones((GLA_CHUNK, GLA_CHUNK), dtype=bool))[None, None, :, :, None]

    def step(s, inp):
        qc, kc, vc, ac = inp
        qf, kf, vf = (t.astype(jnp.float32) for t in (qc, kc, vc))
        b = jnp.cumsum(ac.astype(jnp.float32), axis=2)
        rel = b[:, :, :, None, :] - b[:, :, None, :, :]
        decay = jnp.where(lower_tri, jnp.exp(jnp.minimum(rel, 0.0)), 0.0)
        scores = jnp.einsum('bhid,bhjd,bhijd->bhij', qf, kf, decay)
        o = (jnp.einsum('bhcd,bhde->bhce', qf * jnp.exp(b), s)
             + jnp.einsum('bhij,bhje->bhie', scores, vf))
        b_last = b[:, :, -1:, :]
        s_new = (jnp.exp(b_last[:, :, 0, :])[..., None] * s
                 + jnp.einsum('bhcd,bhce->bhde', kf * jnp.exp(b_last - b), vf))
        return s_new, o.astype(v.dtype)

    s_final, o = lax.scan(step, s0, (chunks(q), chunks(k), chunks(v), chunks(log_a)))
    return o.transpose(1, 2, 0, 3, 4).reshape(b_, h_, l_, dv), s_final

def bidir_gla(q, k, v, a_f, a_b, s0_f, s0_b):
    flip = lambda t: jnp.flip(t, axis=2)
    o_f, s_f = gla_scan(q, k, v, a_f, s0_f)
    o_b, s_b = gla_scan(flip(q), flip(k), flip(v), flip(a_b), s0_b)
    return o_f + flip(o_b), s_f, s_b

def gla_prepare(p, w_gf, b_gf, w_gb, b_gb):
    to_bhld = lambda t, d: heads(t, N_GLA_HEADS, d).transpose(0, 2, 1, 3)
    q = to_bhld(p['gla_q'] * GLA_DK ** -0.5, GLA_DK)
    k = to_bhld(p['gla_k'], GLA_DK)
    v = to_bhld(p['gla_v'], GLA_DV)
    a_f = to_bhld(jax.nn.log_sigmoid((p['gla_gf'] @ w_gf + b_gf).astype(jnp.float32)) / GLA_TAU, GLA_DK)
    a_b = to_bhld(jax.nn.log_sigmoid((p['gla_gb'] @ w_gb + b_gb).astype(jnp.float32)) / GLA_TAU, GLA_DK)
    return q, k, v, a_f, a_b

def gla_output(o, r, gain):
    b_, _, l_, _ = o.shape
    o = rms_norm_2(o.transpose(0, 2, 1, 3), gain).reshape(b_, l_, W_GLA)
    return o * jax.nn.silu(r)

def token_mixing(hx, hz, cos, sin, na_q_norm, na_k_norm, na_rpb, gla_w_gate_f, gla_b_gate_f,
                 gla_w_gate_b, gla_b_gate_b, gla_norm, gqa_q_norm, gqa_k_norm, with_ctx_out):
    px, pz = split_in(hx), split_in(hz)
    b_, s_ = hx.shape[0], hx.shape[1]
    lc = hz.shape[1]
    a_x = fourier_mix(px['fourier'])
    na_q = lambda p: rms_norm_2(heads(p['na_q'], N_NA_HEADS, HEAD_DIM_2), na_q_norm)
    na_k = lambda p: rms_norm_2(heads(p['na_k'], N_NA_HEADS, HEAD_DIM_2), na_k_norm)
    na_v = lambda p: heads(p['na_v'], N_NA_HEADS, HEAD_DIM_2)
    kz_na, vz_na = na_k(pz), na_v(pz)
    b_x = neighborhood_attention(na_q(px), na_k(px), na_v(px), kz_na, vz_na, na_rpb)
    gates = (gla_w_gate_f, gla_b_gate_f, gla_w_gate_b, gla_b_gate_b)
    s0 = jnp.zeros((b_, N_GLA_HEADS, GLA_DK, GLA_DV), jnp.float32)
    oz_gla, s_f, s_b = bidir_gla(*gla_prepare(pz, *gates), s0, s0)
    ox_gla, _, _ = bidir_gla(*gla_prepare(px, *gates), s_f, s_b)
    c_x = gla_output(ox_gla, px['gla_r'], gla_norm)
    gqa_q = lambda p: rms_norm_2(heads(p['gqa_q'], N_GQA_HEADS, HEAD_DIM_2), gqa_q_norm)
    gqa_k = lambda p: rms_norm_2(heads(p['gqa_k'], N_GQA_KV_HEADS, HEAD_DIM_2), gqa_k_norm)
    gqa_v = lambda p: heads(p['gqa_v'], N_GQA_KV_HEADS, HEAD_DIM_2)
    kz_gqa, vz_gqa = gqa_k(pz), gqa_v(pz)
    qx_gqa = apply_rope(gqa_q(px), cos, sin).reshape(b_, s_, N_GQA_KV_HEADS, GQA_GROUP, HEAD_DIM_2)
    kx_gqa = apply_rope(gqa_k(px), cos, sin)
    d_x = block_attention(qx_gqa, jnp.concatenate([kx_gqa, kz_gqa], axis=1),
                          jnp.concatenate([gqa_v(px), vz_gqa], axis=1))
    out_x = jnp.concatenate([a_x, b_x, c_x, d_x], axis=-1)
    if not with_ctx_out:
        return out_x, None
    a_z = fourier_mix(pz['fourier'])
    b_z = block_attention(na_q(pz)[:, :, :, None, :], kz_na, vz_na)
    c_z = gla_output(oz_gla, pz['gla_r'], gla_norm)
    d_z = block_attention(gqa_q(pz).reshape(b_, lc, N_GQA_KV_HEADS, GQA_GROUP, HEAD_DIM_2), kz_gqa, vz_gqa)
    return out_x, jnp.concatenate([a_z, b_z, c_z, d_z], axis=-1)

def second_inputs(seed: int = 0) -> dict:
    key = jax.random.key(seed)
    ks = iter(jax.random.split(key, 32))
    f32 = jnp.float32

    def nrm(shape, std):
        return jax.random.normal(next(ks), shape, f32) * std

    L, D = DEPTH, D_MODEL
    return {
        'x': nrm((BATCH, SEQ, D), 1.0),
        'c': nrm((BATCH, D), 1.0),
        'ctx': nrm((BATCH, CTX_LEN, D), 1.0),
        'c_ctx': nrm((D,), 1.0),
        'w_mod': nrm((L, D, N_MOD * D), 0.5 * D ** -0.5),
        'b_mod': nrm((L, N_MOD * D), 0.02),
        'ffn1_w1': nrm((L, D, D_FF), D ** -0.5),
        'ffn1_w3': nrm((L, D, D_FF), D ** -0.5),
        'ffn1_w2': nrm((L, D_FF, D), D_FF ** -0.5),
        'w_in': nrm((L, D, D_IN), D ** -0.5),
        'na_q_norm': 1.0 + nrm((L, HEAD_DIM_2), 0.1),
        'na_k_norm': 1.0 + nrm((L, HEAD_DIM_2), 0.1),
        'na_rpb': nrm((L, N_NA_HEADS, 2 * NA_ROWS - 1, 2 * NA_COLS - 1), 0.1),
        'gla_w_gate_f': nrm((L, GLA_GATE_RANK, N_GLA_HEADS * GLA_DK), GLA_GATE_RANK ** -0.5),
        'gla_b_gate_f': nrm((L, N_GLA_HEADS * GLA_DK), 0.1),
        'gla_w_gate_b': nrm((L, GLA_GATE_RANK, N_GLA_HEADS * GLA_DK), GLA_GATE_RANK ** -0.5),
        'gla_b_gate_b': nrm((L, N_GLA_HEADS * GLA_DK), 0.1),
        'gla_norm': 1.0 + nrm((L, GLA_DV), 0.1),
        'gqa_q_norm': 1.0 + nrm((L, HEAD_DIM_2), 0.1),
        'gqa_k_norm': 1.0 + nrm((L, HEAD_DIM_2), 0.1),
        'w_out': nrm((L, D_MIX, D), D_MIX ** -0.5),
        'ffn2_w1': nrm((L, D, D_FF), D ** -0.5),
        'ffn2_w3': nrm((L, D, D_FF), D ** -0.5),
        'ffn2_w2': nrm((L, D_FF, D), D_FF ** -0.5),
    }

def second_block(x, c, ctx, c_ctx, w_mod, b_mod, ffn1_w1, ffn1_w3, ffn1_w2, w_in,
              na_q_norm, na_k_norm, na_rpb, gla_w_gate_f, gla_b_gate_f, gla_w_gate_b, gla_b_gate_b,
              gla_norm, gqa_q_norm, gqa_k_norm, w_out, ffn2_w1, ffn2_w3, ffn2_w2):
    cos, sin = axial_rope(x.shape[1])
    z = ctx
    for l in range(DEPTH):
        last = l == DEPTH - 1
        mx = jnp.split((jax.nn.silu(c) @ w_mod[l] + b_mod[l])[:, None, :], N_MOD, axis=-1)
        mz = jnp.split(jax.nn.silu(c_ctx) @ w_mod[l] + b_mod[l], N_MOD, axis=-1)
        x = x + 0.5 * mx[2] * swiglu(modulate(rms_norm_2(x), mx[0], mx[1]), ffn1_w1[l], ffn1_w3[l], ffn1_w2[l])
        z = z + 0.5 * mz[2] * swiglu(modulate(rms_norm_2(z), mz[0], mz[1]), ffn1_w1[l], ffn1_w3[l], ffn1_w2[l])
        hx = modulate(rms_norm_2(x), mx[3], mx[4]) @ w_in[l]
        hz = modulate(rms_norm_2(z), mz[3], mz[4]) @ w_in[l]
        mix_x, mix_z = token_mixing(hx, hz, cos, sin, na_q_norm[l], na_k_norm[l], na_rpb[l],
                                    gla_w_gate_f[l], gla_b_gate_f[l], gla_w_gate_b[l], gla_b_gate_b[l],
                                    gla_norm[l], gqa_q_norm[l], gqa_k_norm[l], not last)
        x = x + mx[5] * (mix_x @ w_out[l])
        x = x + 0.5 * mx[8] * swiglu(modulate(rms_norm_2(x), mx[6], mx[7]), ffn2_w1[l], ffn2_w3[l], ffn2_w2[l])
        if not last:
            z = z + mz[5] * (mix_z @ w_out[l])
            z = z + 0.5 * mz[8] * swiglu(modulate(rms_norm_2(z), mz[6], mz[7]), ffn2_w1[l], ffn2_w3[l], ffn2_w2[l])
    return x


def setup_inputs(seed=0):
    out = dict(first_inputs(seed))
    for name, value in second_inputs(seed + 1).items():
        if name != "x":
            out[name + "_2"] = value
    return out


def reference(
    x, norm1_g, w_in, q_norm_g, k_norm_g, w_attn_out, conf_conv_w, conf_conv_b, conf_ln_g,
    conf_ln_b, w_conf_out, sc_conv_w, w_sc_out, w_o, norm2_g, w_up, ffn_conv_w, ffn_conv_b,
    w_down, c_2, ctx_2, c_ctx_2, w_mod_2, b_mod_2, ffn1_w1_2, ffn1_w3_2, ffn1_w2_2, w_in_2,
    na_q_norm_2, na_k_norm_2, na_rpb_2, gla_w_gate_f_2, gla_b_gate_f_2, gla_w_gate_b_2,
    gla_b_gate_b_2, gla_norm_2, gqa_q_norm_2, gqa_k_norm_2, w_out_2, ffn2_w1_2, ffn2_w3_2,
    ffn2_w2_2,
):
    x = first_block(
        x, norm1_g, w_in, q_norm_g, k_norm_g, w_attn_out, conf_conv_w, conf_conv_b, conf_ln_g,
        conf_ln_b, w_conf_out, sc_conv_w, w_sc_out, w_o, norm2_g, w_up, ffn_conv_w, ffn_conv_b,
        w_down,
    )
    return second_block(
        x, c_2, ctx_2, c_ctx_2, w_mod_2, b_mod_2, ffn1_w1_2, ffn1_w3_2, ffn1_w2_2, w_in_2,
        na_q_norm_2, na_k_norm_2, na_rpb_2, gla_w_gate_f_2, gla_b_gate_f_2, gla_w_gate_b_2,
        gla_b_gate_b_2, gla_norm_2, gqa_q_norm_2, gqa_k_norm_2, w_out_2, ffn2_w1_2, ffn2_w3_2,
        ffn2_w2_2,
    )


_drawn_inputs = setup_inputs


def setup_inputs(seed=0):
    import zlib

    import numpy as np

    out = dict(_drawn_inputs(seed))
    spreads = {}
    factors = {'q_norm_g': 6.402,
     'k_norm_g': 6.369,
     'conf_conv_b': 4.947,
     'conf_ln_b': 8.0,
     'ffn_conv_b': 4.998,
     'ctx_2': 2.877,
     'b_mod_2': 3.529,
     'na_q_norm_2': 8.0,
     'na_k_norm_2': 8.0,
     'na_rpb_2': 64.0,
     'gla_w_gate_f_2': 4.95,
     'gla_b_gate_f_2': 8.0,
     'gla_w_gate_b_2': 5.601,
     'gla_b_gate_b_2': 8.0,
     'gla_norm_2': 6.219,
     'gqa_q_norm_2': 8.0,
     'gqa_k_norm_2': 8.0}
    for name, (base, spread) in spreads.items():
        noise = np.random.default_rng([zlib.crc32(name.encode()), seed]).standard_normal(out[name].shape)
        drawn = base * np.exp(spread * noise) if base else spread * noise
        out[name] = jnp.asarray(drawn.astype(out[name].dtype))
    for name, factor in factors.items():
        out[name] = (out[name] * factor).astype(out[name].dtype)
    return out
```

```python
from contextlib import ExitStack

import numpy as np

import concourse.bass as bass
from concourse import mybir
from concourse.alu_op_type import AluOpType as ALU

ACT = mybir.ActivationFunctionType
F32 = mybir.dt.float32
AX_X = mybir.AxisListType.X

P = 128
D = 1024
KT = D // P
S = 256
TT = S // P
DEPTH = 2
HEADS, KV_HEADS, HD = 8, 2, 128
IDX_HEADS, IDX_DIM, TOP_K = 8, 64, 64
CONV_K, SC_K, FFN_K = 31, 3, 3
FFN = 2816
FT = FFN // P
EPS = 1e-6
NMOD = 9
HD2 = 64
GLA_LEVELS = 8
TAU = 16.0
NEG = -1.0e30
TAKEN = -3.0e38

BANKS = 8
BANK = 512
SLOTS = 4
ARENA = 25096
SLOT = 3072

_w = [HEADS * HD, KV_HEADS * HD, KV_HEADS * HD, IDX_HEADS * IDX_DIM, IDX_DIM, IDX_HEADS, 2 * D, 3 * D, 3 * D]
Q0, K0, V0, IQ0, IK0, IW0, A0, C0, G0 = np.cumsum([0] + _w)[:-1].tolist()
_w2 = [256, 256, 256, 256, 128, 128, 256, 256, 16, 16, 256, 128, 128]
F20, NQ0, NK0, NV0, GQ0, GK0, GV0, GR0, GF0, GB0, AQ0, AK0, AV0 = np.cumsum([0] + _w2)[:-1].tolist()

P1 = {}
_at = 0
for _n, _c in (("norm1", KT), ("norm2", KT), ("qg", 1), ("kg", 1), ("conf_w", KT * CONV_K), ("conf_b", KT),
               ("ln_g", KT), ("ln_b", KT), ("sc_w", KT * SC_K), ("ffn_w", 2 * FT * FFN_K), ("ffn_b", 2 * FT)):
    P1[_n] = _at
    _at += _c
P1_COLS = _at
P2 = {}
_at = 0
for _n, _c in (("b_mod", NMOD * KT), ("na_q", 1), ("na_k", 1), ("gla_n", 1), ("gqa_q", 1), ("gqa_k", 1),
               ("gate_f", 1), ("gate_b", 1)):
    P2[_n] = _at
    _at += _c
P2_COLS = _at

CONST = {}
_at = 0
for _n, _c in (("ident", P), ("ones", P), ("rot_q", P), ("rot_i", P), ("rot_g", P), ("ones64", P), ("flip", P),
               ("cos_q", S), ("sin_q", S), ("cos_i", S), ("sin_i", S), ("cos_g", S), ("sin_g", S),
               ("causal0", P), ("causal1", S), ("level", GLA_LEVELS * P), ("window", TT * S),
               ("dft_d", 2 * P), ("sel", 2), ("cos_l", TT * S), ("sin_l", TT * S)):
    CONST[_n] = (_at, _c)
    _at += _c
CONST_COLS = _at


def shape_constants():
    c = {}
    c["ident"] = np.eye(P)
    c["ones"] = np.ones((P, P))
    row = np.arange(P)

    def rotation(block, half):
        r = np.zeros((P, P))
        for i in range(P):
            j = i % block
            if j < half:
                r[i + half, i] = -1.0
            elif j < 2 * half:
                r[i - half, i] = 1.0
        return r

    def tables(block, half, angle):
        cos, sin = np.ones((P, S)), np.zeros((P, S))
        for i in range(P):
            j = i % block
            if j < 2 * half:
                cos[i], sin[i] = np.cos(angle[:, j % half]), np.sin(angle[:, j % half])
        return cos, sin

    pos = np.arange(S, dtype=np.float64)
    for name, block, rot in (("q", HD, HD // 4), ("i", IDX_DIM, IDX_DIM // 4)):
        inv = 500000.0 ** (-np.arange(0, rot, 2) / rot)
        c["rot_" + name] = rotation(block, rot // 2)
        c["cos_" + name], c["sin_" + name] = tables(block, rot // 2, pos[:, None] * inv)
    nf = HD2 // 4
    inv = 10000.0 ** (-np.arange(nf) / nf)
    angle = np.concatenate([(pos // 64)[:, None] * inv, (pos % 64)[:, None] * inv], axis=1)
    c["rot_g"] = rotation(HD2, HD2 // 2)
    c["cos_g"], c["sin_g"] = tables(HD2, HD2 // 2, angle)
    c["ones64"] = (row[:, None] // HD2 == row[None, :] // HD2) * 1.0
    c["flip"] = np.kron(np.eye(2), np.eye(HD2)[::-1])
    c["causal0"] = np.where(row[None, :] <= row[:, None], 0.0, NEG)
    c["causal1"] = np.concatenate([np.zeros((P, P)), c["causal0"]], axis=1)
    levels = []
    for lv in range(1, GLA_LEVELS):
        m = P >> lv
        same = row[:, None] // (2 * m) == row[None, :] // (2 * m)
        levels.append(same & (row[:, None] // m != row[None, :] // m))
    levels.append(2.0 * np.eye(P))
    c["level"] = np.concatenate([x * 1.0 for x in levels], axis=1)
    t = np.arange(S)
    start = np.clip(t % 64 - 8, 0, 64 - 16)
    seen = (t[None, :] % 64 >= start[:, None]) & (t[None, :] % 64 < start[:, None] + 16)
    c["window"] = np.where(seen, 0.0, NEG).reshape(TT, P, S).transpose(1, 0, 2).reshape(P, TT * S)
    d = np.arange(HD2)
    a = 2 * np.pi * np.outer(d, d) / HD2
    two = lambda m: np.kron(np.eye(2), m)
    c["dft_d"] = np.concatenate([two(np.cos(a)), two(np.sin(a))], axis=1) / np.sqrt(S * HD2)
    c["sel"] = (row[:, None] % 32 == np.arange(2)[None, :]) * 1.0
    a = 2 * np.pi * np.outer(t, t) / S
    fold = lambda m: m.reshape(TT, P, S).transpose(1, 0, 2).reshape(P, TT * S)
    c["cos_l"], c["sin_l"] = fold(np.cos(a)), fold(-np.sin(a))
    return np.concatenate([c[n] for n in CONST], axis=1).astype(np.float32)


class Plan:

    def __init__(self):
        self.steps = []
        self.number = {}
        self.chunks = []
        self.last_job = {}

    def step(self, kind, l, *a):
        self.steps.append((kind, l, *a))

    def job(self, *name, chunk=None):
        self.number[name] = len(self.number)
        if chunk is not None:
            if chunk not in self.last_job:
                self.chunks.append(chunk)
            self.last_job[chunk] = self.number[name]


def mod_step(p, l, c):
    if c < NMOD * KT // 2:
        p.step("mod", l, c)
        p.job("mod", l, c, chunk=("mod", l, c))
    if c:
        p.step("mod_t", l, c - 1)
        p.job("mod_t", l, c - 1)


def plan_first(p, l):
    mods = iter(range(NMOD * KT // 2 + 1))

    def mod(n):
        for _ in range(n):
            c = next(mods, None)
            if c is not None:
                mod_step(p, l, c)

    def norm(n):
        p.step("norm", l, n)
        p.job("ss", l, n)

    norm(0)
    nqk = HEADS + KV_HEADS
    for i in range(nqk + 2):
        if i < nqk:
            p.step("qk", l, i)
            p.job("qk", l, i, chunk=("qk", l, i // 2))
        if 1 <= i < nqk + 1:
            p.step("qss", l, i - 1)
            p.job("qss", l, i - 1)
        if 2 <= i:
            p.step("qrot", l, i - 2)
            p.job("qrot", l, i - 2)
        if i == nqk:
            for t in range(TT):
                p.step("v", l, t)
                p.job("v", l, t, chunk=("v", l))
    for i in range(6):
        if i < 5:
            p.step("iq", l, i)
            p.job("iq", l, i, chunk=("iq", l, i // 2))
        if i == 4:
            for t in range(TT):
                p.step("iw", l, t)
                p.job("iw", l, t, chunk=("iq", l, 2))
        if i >= 1:
            p.step("irot", l, i - 1)
            p.job("irot", l, i - 1)
    for t in range(TT):
        for h in range(IDX_HEADS):
            p.step("idx", l, t, h)
            p.job("idx", l, t, h)
    conv = [(i, n) for i in range(KT) for n in range(4)]
    for i in range(KT):
        p.step("a", l, i)
        p.job("agate", l, i, chunk=("a", l, i))
        p.job("aval", l, i, chunk=("a", l, i))
        if i == 0:
            p.step("topk", l, 0)
        elif i == 2:
            p.step("topk", l, 1)
        elif conv[0][0] < i:
            p.step("conv", l, *conv.pop(0))
        mod(1)
    units = [(h, t) for h in range(HEADS) for t in range(TT)]

    def att_front(n):
        if n < len(units):
            p.step("att", l, *units[n])
            p.job("att", l, *units[n])

    def att_norm(n):
        if 0 <= n < len(units):
            p.step("att_n", l, *units[n])

    def att_back(n):
        if 0 <= n < len(units):
            p.step("att_t", l, *units[n])
            p.job("att_t", l, *units[n])

    def att_out(hd):
        if 0 <= hd < HEADS:
            p.step("att_o", l, hd)
            p.job("att_o", l, hd)

    for i in range(KT + 1):
        parts = ("cc", "cx", "cb") if i < KT else ()
        att_front(2 * i)
        for n, part in enumerate(parts or (None, None, None)):
            if part:
                p.step(part, l, i)
                p.job(part, l, i, chunk=("c", l, i))
            else:
                p.step("g", l, n)
                p.job("g", l, n, chunk=("g", l, n // 2))
            if n == 0:
                att_norm(2 * i - 1)
                att_back(2 * i - 2)
                att_front(2 * i + 1)
            elif n == 1:
                att_norm(2 * i)
                att_back(2 * i - 1)
                if conv:
                    p.step("conv", l, *conv.pop(0))
        att_out(i - 1)
        mod(1)
    for g in range(3, 24):
        p.step("g", l, g)
        p.job("g", l, g, chunk=("g", l, g // 2))
        if conv:
            p.step("conv", l, *conv.pop(0))
        if g % 2:
            mod(1)
    while conv:
        p.step("conv", l, *conv.pop(0))
    p.step("mean", l)
    p.job("mean", l)
    for i in range(KT):
        p.step("sc_out", l, i)
        p.job("sc_out", l, i, chunk=("sc_out", l, i // 2))
    p.step("var", l)
    p.job("var", l)
    for i in range(KT):
        p.step("att_out", l, i)
        p.job("att_out", l, i, chunk=("att_out", l, i // 2))
    for i in range(KT):
        p.step("conf_out", l, i)
        p.job("conf_out", l, i, chunk=("conf_out", l, i // 2))
    for i in range(KT):
        p.step("wo", l, i)
        p.job("wo", l, i, chunk=("wo", l, i // 2))
    norm(1)
    for i in range(FT + 1):
        if i < FT:
            p.step("up", l, i)
            p.job("up", l, i, 0, chunk=("up", l, i))
            p.job("up", l, i, 1, chunk=("up", l, i))
            if i % 2:
                mod(1)
        if i >= 1:
            p.step("up_act", l, i - 1)
    for i in range(KT):
        p.step("down", l, i)
        p.job("down", l, i, chunk=("down", l, i))
    mod(NMOD * KT // 2 + 1)
    p.step("mod_fin", l)


def mix_units(last):
    groups = [("gqa", 0)] + ([] if last else [("gqa", 1), ("na", 1)]) + [("na", 0)]
    return [(kind, s, h, t) for kind, s in groups for h in range(4) for t in range(TT)]


def plan_second(p, l):
    last = l == DEPTH - 1

    def norm(n):
        p.step("norm2", l, n)
        p.job("ss2", l, n)

    def ffn(w):
        for i in range(FT):
            p.step("f1", l, w, i)
            p.job("f1", l, w, i, chunk=("f1", l, w, i))
            p.job("f3", l, w, i, chunk=("f1", l, w, i))
        for i in range(KT):
            p.step("f2", l, w, i)
            p.job("f2", l, w, i, chunk=("f2", l, w, i))

    norm(0)
    ffn(0)
    norm(1)
    p.step("gate_in", l)
    p.job("gate_in", l, chunk=("w2", l, "gk"))
    order = [6, 4, 5, 0, 1, 2, 3]
    chunk_of = {6: "gk", 4: "gq", 5: "gq", 0: "naq", 1: "naq", 2: "nak", 3: "nak"}
    for n in range(len(order) + 2):
        if n < len(order):
            p.step("np", l, n, order[n])
            p.job("np", l, n, chunk=("w2", l, chunk_of[order[n]]))
        if n == 0:
            for d in range(2):
                p.step("gate", l, d)
                p.job("gate", l, d)
        if 1 <= n <= len(order):
            p.step("nss", l, n - 1, order[n - 1])
            p.job("nss", l, n - 1)
        if 2 <= n and order[n - 2] >= 4:
            p.step("nrot", l, n - 2, order[n - 2])
            p.job("nrot", l, n - 2)
    for i in range(2):
        p.step("gp", l, i)
        p.job("gp", l, i, chunk=("w2", l, "glaqk"))
    for t in range(2 * TT):
        p.step("gv", l, t)
        p.job("gv", l, t, chunk=("w2", l, "glav"))
    for s in (1, 0):
        if s == 1:
            p.step("g_exp", l, 1)
            for i in range(2):
                p.step("rp", l, i)
                p.job("rp", l, i, chunk=("w2", l, "glar"))
            for t in range(2 * TT):
                p.step("vp", l, t)
                p.job("vp", l, t, chunk=("w2", l, "v"))
            for i in range(2):
                p.step("fp", l, i)
                p.job("fp", l, i, chunk=("w2", l, "four"))
            p.step("g_kt", l)
            p.job("g_kt", l)
            for d in range(2):
                p.step("g_s0", l, d)
                p.job("g_s0", l, d)
            if last:
                continue
        else:
            p.step("g_exp", l, 0)
            for s2 in range(1 if last else 2):
                for t in range(TT):
                    p.step("four1", l, s2, t)
                    p.job("four1", l, s2, t)
                for g in range(2):
                    p.step("four2", l, s2, g)
                    p.job("four2", l, s2, g)
        for hd in range(4):
            p.step("g_x", l, s, hd)
            p.job("g_x", l, s, hd)
            for lp in range(GLA_LEVELS // 2):
                p.step("g_lv", l, s, hd, lp)
                p.job("g_lv", l, s, hd, lp)
        for pr in range(2):
            p.step("g_o", l, s, pr)
            p.job("g_o", l, s, pr)
        for pr in range(2):
            p.step("g_n", l, s, pr)
            p.job("g_n", l, s, pr)
    units = mix_units(last)
    p.step("na_load", l)
    for n in range(len(units) + 4):
        if n == len(units) - 8:
            p.step("na_bias", l)
            for hd in range(4):
                p.job("flip", l, hd)
        if n < len(units):
            p.step("at", l, n)
            p.job("at", l, n)
        if 1 <= n <= len(units):
            p.step("at_n", l, n - 1)
        if 2 <= n < len(units) + 2:
            p.step("at_t", l, n - 2)
            p.job("at_t", l, n - 2)
        if n >= 4 and n % 2 == 0:
            p.step("at_o", l, n - 4)
            p.job("at_o", l, n - 4)
    for i in range(KT):
        p.step("out", l, i)
        p.job("out", l, i, chunk=("out", l, i // 2))
    norm(2)
    ffn(1)


def build(nc, a, out):
    plan = Plan()
    for l in range(DEPTH):
        plan_first(plan, l)
    for l in range(DEPTH):
        plan_second(plan, l)
    job = plan.number
    steps = plan.steps

    with ExitStack() as ctx:
        def sb(name, cols):
            return ctx.enter_context(nc.sbuf_tensor(name, [P, cols], F32))

        def sem(name):
            return ctx.enter_context(nc.semaphore(name))

        psum = ctx.enter_context(nc.psum_tensor("psum", [P, BANKS, BANK], F32))

        consts = sb("consts", CONST_COLS)
        par1 = sb("par1", DEPTH * P1_COLS)
        par2 = sb("par2", DEPTH * P2_COLS)
        ring = sb("ring", SLOTS * SLOT)
        xz = sb("xz", KT * 2 * S)
        hh = sb("hh", KT * 2 * S)
        small = sb("small", 3 * 8 + 8 * 2 + 8)
        mods = sb("mods", DEPTH * NMOD * KT * 2)
        gate_w = sb("gate_w", DEPTH * 2 * P)
        arena = sb("arena", ARENA)

        def const(name):
            at, n = CONST[name]
            return consts[:, at:at + n]

        ident, ones, ones64 = const("ident"), const("ones"), const("ones64")

        def par(name, l, i=0):
            c = l * P1_COLS + P1[name] + i
            return par1[:, c:c + 1]

        def pr2(name, l, i=0):
            c = l * P2_COLS + P2[name] + i
            return par2[:, c:c + 1]

        x = xz[:, :].rearrange("p (k t) -> p k t", k=KT)
        h = hh[:, :].rearrange("p (k t) -> p k t", k=KT)
        slots = ring[:, :].rearrange("p (s c) -> p s c", s=SLOTS)
        mod = mods[:, :].rearrange("p (l f s) -> p l f s", l=DEPTH, s=2)
        gw = gate_w[:, :].rearrange("p (l d c) -> p l d c", l=DEPTH, d=2)
        eps_c = small[:, 0:1]
        craw = small[:, 24:40].rearrange("p (k s) -> p k s", s=2)
        stat = small[:, 1:8]

        class Carve:
            def __init__(self, base=0):
                self.at = base

            def __call__(self, *dims):
                n = int(np.prod(dims))
                v = arena[:, self.at:self.at + n]
                self.at += n
                assert self.at <= ARENA, self.at
                if len(dims) == 2:
                    v = v.rearrange("p (a b) -> p a b", a=dims[0])
                if len(dims) == 3:
                    v = v.rearrange("p (a b c) -> p a b c", a=dims[0], b=dims[1])
                if len(dims) == 4:
                    v = v.rearrange("p (a b c d) -> p a b c d", a=dims[0], b=dims[1], c=dims[2])
                return v

        wide = arena[:, 0:FT * 2 * S]
        act1 = wide[:, 0:FT * S].rearrange("p (k t) -> p k t", k=FT)
        act2 = wide.rearrange("p (k t) -> p k t", k=FT)
        gates = wide[:, 0:24 * S].rearrange("p (k t) -> p k t", k=24)
        sq1 = wide[:, 24 * S:32 * S].rearrange("p (k t) -> p k t", k=KT)
        attn = x[:, :, S:2 * S]
        scv = h[:, :, S:2 * S]
        c = Carve(32 * S)
        sqb = c(2, S)
        raw = c(3, S)
        sdb = c(2, S)
        qn = c(2, S)
        tmp = c(S)
        iraw = c(2, S)
        up_buf = arena[:, 32 * S:36 * S].rearrange("p (b u t) -> p b u t", b=2, u=2)
        c = Carve(FT * 2 * S)
        rs = c(2 * S)
        sd = c(2 * S)
        after_norm = c.at
        qk_t = c(HEADS + KV_HEADS, S)
        merged = qk_t
        v_tok = c(TT, KV_HEADS * HD)
        iq_t = c(5, S)
        iw_s = c(TT, IDX_HEADS)
        aval = c(KT, S)
        aconv = c(KT, S)
        rel = raw
        csil = c(KT, 32)
        mod_part = iraw
        score = c(TT, S)
        work = c(S)
        top8 = small[:, 40:48]
        mbias = c(TT, S)
        lg = c(2, S)
        pe_ = c(2, S)
        pn = c(2, S)
        pt = c(2, TT, S)
        sg, cct, cbt = qn, sqb, sdb
        tmpc = work
        c = Carve(after_norm)
        silu2 = c(2, 2 * S)
        sq2 = c(KT, 2 * S)
        c = Carve(0)
        nq = c(7, 2 * S)
        glaqk = c(2, 2 * S)
        r_t = c(2, 2 * S)
        vtok = c(2 * TT, 384)
        glav = c(2 * TT, 256)
        four = c(2, 2 * S)
        la = c(2, 2 * S)
        fab = c(TT, 2, 2, P)
        assert c.at <= FT * 2 * S
        c = Carve(after_norm)
        sqb2 = c(2, 2 * S)
        raw2 = c(2, 2 * S)
        sd2 = c(2, 2 * S)
        tmp2 = c(2 * S)
        union = c.at
        g32 = c(2 * S)
        gabs = c(2 * S)
        c = Carve(union)
        cum_f = c(S)
        cum_b = c(S + 1)
        c(1)
        expo = c(20, S)
        at_m = c(4, 2 * TT, P)
        k_tok = c(2, TT, P)
        s0 = c(2, 256)
        gtmp, gacc = sqb2[:, :, S:2 * S], raw2[:, :, S:2 * S]
        c = Carve(union)
        nab = c(4, TT, S)
        p2 = c(2, 2 * S)
        pn2 = c(2, 2 * S)
        pt2 = c(2, 4, S)
        nab_raw = c(4, TT, S)
        mixt = h

        product_done = sem("product_done")
        bank_free = [sem(f"bank{b}_free") for b in range(BANKS)]
        loaded = [sem(f"slot{s}_loaded") for s in range(SLOTS)]
        x_in, inputs_in = sem("x_in"), sem("inputs_in")
        context_in = sem("context_in")
        bias_in = sem("bias_in")
        small_ready = sem("small_ready")
        c_ready = sem("c_ready")
        scalar_step, vector_step, pool_step = sem("scalar_step"), sem("vector_step"), sem("pool_step")
        x_squared, h_ready = sem("x_squared"), sem("h_ready")
        qk_normed, qk_roped, idx_roped, idx_summed = sem("qk_normed"), sem("qk_roped"), sem("idx_roped"), sem("idx_summed")
        conv_done, centered, c_squared, ln_scaled, conf_ready = (sem("conv_done"), sem("centered"), sem("c_squared"),
                                                                 sem("ln_scaled"), sem("conf_ready"))
        max_ready, exp_done, p_normed = sem("max_ready"), sem("exp_done"), sem("p_normed")
        sc_ready, merged_ready = sem("sc_ready"), sem("merged_ready")
        up_seeded, up_silu, act_ready = sem("up_seeded"), sem("up_silu"), sem("act_ready")
        mod_ready = sem("mod_ready")
        x2_squared, x2_scaled, h2_ready = sem("x2_squared"), sem("x2_scaled"), sem("h2_ready")
        n_normed, n_roped = sem("n_normed"), sem("n_roped")
        gate_abs, gate_log, decay_log = sem("gate_abs"), sem("gate_log"), sem("decay_log")
        exponents, decays, q_decayed, k_decayed = sem("exponents"), sem("decays"), sem("q_decayed"), sem("k_decayed")
        level_added, gla_ready = sem("level_added"), sem("gla_ready")
        bias_ready = sem("bias_ready")
        max2_ready, exp2_done, p2_normed = sem("max2_ready"), sem("exp2_done"), sem("p2_normed")
        out_done = sem("out_done")

        def bank(j):
            return psum[:, j % BANKS, :]

        def freed(j):
            return j // BANKS + 1

        def produced(eng, j):
            eng.wait_ge(product_done, j + 1)

        def evacuated(eng, j):
            eng.wait_ge(bank_free[j % BANKS], freed(j))

        def last_job(kind, l, *rest):
            return job[(kind, l, *rest)]

        def rows(w):
            return w.rearrange("(k p) n -> p k n", p=P)

        def pieces(name):
            kind, l = name[:2]
            cols = []
            if kind in ("qk", "v", "iq", "a", "c", "g"):
                w = rows(a["w_in"][l])
                i = name[2] if len(name) > 2 else 0
                if kind == "qk":
                    cols = [(Q0 + 256 * i, 256)]
                elif kind == "v":
                    cols = [(V0, 256)]
                elif kind == "iq":
                    cols = [(IQ0 + 256 * i, 256)] if i < 2 else [(IK0, IDX_DIM), (IK0, IDX_DIM + IDX_HEADS)]
                elif kind == "a":
                    cols = [(A0 + D + P * i, P), (A0 + P * i, P)]
                elif kind == "c":
                    cols = [(C0 + D + P * i, P), (C0 + 2 * D + P * i, P), (C0 + P * i, P)]
                elif kind == "g":
                    cols = [(G0 + 256 * i, 256)]
                src = [(w, c0, n) for c0, n in cols]
            elif kind in ("sc_out", "att_out", "conf_out", "wo", "out"):
                w = {"sc_out": "w_sc_out", "att_out": "w_attn_out", "conf_out": "w_conf_out", "wo": "w_o",
                     "out": "w_out_2"}[kind]
                src = [(rows(a[w][l]), 256 * name[2], 256)]
            elif kind == "up":
                w = rows(a["w_up"][l])
                src = [(w, P * name[2], P), (w, FFN + P * name[2], P)]
            elif kind == "down":
                src = [(rows(a["w_down"][l]), P * name[2], P)]
            elif kind == "mod":
                src = [(rows(a["w_mod_2"][l]), 256 * name[2], 256)]
            elif kind == "f1":
                n = name[2] + 1
                src = [(rows(a[f"ffn{n}_w1_2"][l]), P * name[3], P), (rows(a[f"ffn{n}_w3_2"][l]), P * name[3], P)]
            elif kind == "f2":
                src = [(rows(a[f"ffn{name[2] + 1}_w2_2"][l]), P * name[3], P)]
            elif kind == "w2":
                w = rows(a["w_in_2"][l])
                cols = {"four": [(F20, 256)], "naq": [(NQ0, 256)], "nak": [(NK0, 256)], "gq": [(AQ0 + HD2 * q, HD2) for q in (0, 2, 1, 3)],
                        "gk": [(AK0, 128), (GF0, 32)], "glaqk": [(GQ0, 256)], "glar": [(GR0, 256)],
                        "glav": [(GV0, 256)], "v": [(NV0, 256), (AV0, 128)]}[name[2]]
                src = [(w, c0, n) for c0, n in cols]
            kt = FT if kind in ("down", "f2") else KT
            return kt, sum(n for _, _, n in src), src

        slot_of, ready_at = {}, {}
        total = [0] * SLOTS
        for n, name in enumerate(plan.chunks):
            slot_of[name] = n % SLOTS
            total[n % SLOTS] += 16 * len(pieces(name)[2])
            ready_at[name] = total[n % SLOTS]

        def weights(name):
            kt, width, _ = pieces(name)
            return slots[:, slot_of[name], 0:kt * width].rearrange("p (k c) -> p k c", k=kt)

        def unit_before(hd, t, d):
            n = hd * TT + t - d
            return n // TT, n % TT

        def gla_count(l, done):
            return 4 * l + (4 if l < DEPTH - 1 else 2)

        def gla_index(l, s, pr):
            return 4 * l + (0 if (s == 1 or l == DEPTH - 1) else 2) + pr

        def exp_index(l, s):
            return 2 * l + (0 if s == 1 else 1)

        def at_index(l, n):
            return l * len(mix_units(False)) + n

        def toeplitz(eng, l):
            rpb = a["na_rpb_2"]
            for hd in range(4):
                for row in range(4):
                    base = ((l * 4 + hd) * 15 + 7 - row) * 31 + 15 - 63
                    src = bass.AP(tensor=rpb.tensor, offset=base, ap=[[1, 64], [31, 4], [1, 64]])
                    dst = nab_raw[64 * (row % 2):64 * (row % 2) + 64, hd, row // 2, :].rearrange("p (j c) -> p j c", j=4)
                    eng.dma_start(dst, src).then_inc(bias_in, 16)

        def tokens(l, n):
            return S if l == DEPTH - 1 and n == 2 else 2 * S

        def n_tokens(l, i):
            return S if l == DEPTH - 1 and i in (0, 1, 4, 5) else 2 * S

        def scaled_count(l, n, k, s):
            before = 2 * KT * (3 * l + n)
            return before + k * (tokens(l, n) // S) + s + 1

        def h2_tiles(l, n):
            return h2_ready, scaled_count(l, n, 0, 0) - 1, tokens(l, n) // S

        def h2_count(l, n):
            return scaled_count(l, n, KT - 1, tokens(l, n) // S - 1)

        def kdec(l, s):
            return 2 * l + (1 if s == 1 or l == DEPTH - 1 else 2)

        def lev(l, s, hd):
            return 8 * l + (0 if s == 1 or l == DEPTH - 1 else 4) + hd + 1

        block = ctx.enter_context(nc.Block())

        @block.sync
        def _(sp):
            for n, name in enumerate(plan.chunks):
                if n >= SLOTS:
                    sp.wait_ge(product_done, plan.last_job[plan.chunks[n - SLOTS]] + 1)
                at = 0
                for w, c0, cols in pieces(name)[2]:
                    sp.dma_start(weights(name)[:, :, at:at + cols], w[:, :, c0:c0 + cols]).then_inc(loaded[n % SLOTS], 16)
                    at += cols
            for i in range(KT):
                evacuated(sp, last_job("f2", DEPTH - 1, 1, i))
                sp.dma_start(out.rearrange("(k p) t -> p k t", p=P)[:, i, :], x[:, i, 0:S]).then_inc(out_done, 16)
            sp.wait_ge(out_done, 16 * KT)

        @block.gpsimd
        def _(pool):
            n_step = [0]

            def do(ins):
                n_step[0] += 1
                ins.then_inc(pool_step, 1)
                pool.wait_ge(pool_step, n_step[0])

            for kind, l, *r in steps:
                if kind == "norm2" and (l, r[0]) == (0, 0):
                    evacuated(pool, last_job("down", DEPTH - 1, KT - 1))
                    pool.dma_start(x[:, :, S:2 * S], a["ctx"].rearrange("(k p) t -> p k t", p=P)).then_inc(context_in, 16)
                elif kind == "na_load":
                    pool.wait_ge(gla_ready, gla_count(l, True))
                    toeplitz(pool, l)
                elif kind == "g_exp" and not (l == DEPTH - 1 and r[0] == 1):
                    n = exp_index(l, r[0])
                    pool.wait_ge(decays, n + 1)
                    s = r[0]
                    nslots = 8
                    e = expo[:, 0:nslots, :]
                    q = glaqk[:, 0:1, s * S:(s + 1) * S]
                    do(pool.tensor_tensor(e, e, q.to_broadcast([P, nslots, S]), ALU.mult))
                    if s == 0:
                        pool.tensor_tensor(expo[:, 16:18, :], expo[:, 16:18, :], q.to_broadcast([P, 2, S]),
                                           ALU.mult).then_inc(q_decayed, 1)
                    else:
                        pool.tensor_tensor(expo[:, 18:20, :], expo[:, 18:20, :],
                                           glaqk[:, 1:2, S:2 * S].to_broadcast([P, 2, S]),
                                           ALU.mult).then_inc(q_decayed, 1)
                    pool.wait_ge(q_decayed, n + 1)
                elif kind == "g_exp":
                    n = exp_index(l, 1)
                    pool.wait_ge(decays, n + 1)
                    pool.tensor_tensor(expo[:, 18:20, :], expo[:, 18:20, :],
                                       glaqk[:, 1:2, S:2 * S].to_broadcast([P, 2, S]), ALU.mult).then_inc(q_decayed, 1)
                    pool.wait_ge(q_decayed, n + 1)

        @block.scalar
        def _(act):
            n_step = [0]

            def do(ins, s=None, v=None):
                if s is None:
                    n_step[0] += 1
                    s, v = scalar_step, n_step[0]
                ins.then_inc(s, 1)
                act.wait_ge(s, v)

            def free(ins, j):
                do(ins, bank_free[j % BANKS], freed(j))

            x_dram = a["x"].rearrange("(k p) t -> p k t", p=P)
            first = 2 * P
            act.dma_start(x[:, :, 0:S], x_dram).then_inc(x_in, 16)
            act.dma_start(consts[:, 0:first], a["consts"][:, 0:first]).then_inc(x_in, 16)
            act.dma_start(consts[:, first:], a["consts"][:, first:]).then_inc(inputs_in, 16)
            act.dma_start(par1[:, :].rearrange("p (l c) -> p l c", l=DEPTH),
                           a["par1"].rearrange("l p c -> p l c")).then_inc(inputs_in, 16)
            act.dma_start(par2[:, :].rearrange("p (l c) -> p l c", l=DEPTH),
                           a["par2"].rearrange("l p c -> p l c")).then_inc(inputs_in, 16)
            act.dma_start(craw, a["c2"].rearrange("(k p) s -> p k s", p=P)).then_inc(inputs_in, 16)
            act.dma_start(gw[0:32], a["gate_w"].rearrange("l d r c -> r l d c")).then_inc(inputs_in, 16)
            act.wait_ge(x_in, 32)
            act.wait_ge(small_ready, 1)
            for kind, l, *r in steps:
                if kind == "norm":
                    n = l * 2 + r[0]
                    for g in range(KT):
                        if r[0] == 0 and l > 0:
                            evacuated(act, job[("down", l - 1, g)])
                        elif r[0] == 1:
                            evacuated(act, job[("wo", l, g)])
                        nc.scalar.activation(sq1[:, g, :], x[:, g, 0:S], ACT.Square).then_inc(x_squared, 1)
                    act.wait_ge(x_squared, (n + 1) * KT)
                    j = job[("ss", l, r[0])]
                    produced(act, j)
                    free(nc.scalar.activation(sd[:, 0:S], bank(j)[:, 0:S], ACT.Sqrt, scale=1.0 / D, bias=eps_c), j)
                    if n == 0:
                        act.wait_ge(inputs_in, 80)
                        do(nc.scalar.activation(csil[:, :, 0:2], craw, ACT.Silu), c_ready, 1)
                elif kind == "qk":
                    i, j = r[0], job[("qk", l, r[0])]
                    n = l * (HEADS + KV_HEADS) + i
                    produced(act, j)
                    do(nc.scalar.activation(sqb[:, i % 2, :], bank(j)[:, 0:S], ACT.Square))
                    if i >= 3:
                        act.wait_ge(qk_normed, n - 2)
                    free(nc.scalar.activation(raw[:, i % 3, :], bank(j)[:, 0:S], ACT.Copy), j)
                elif kind == "qss":
                    i, j = r[0], job[("qss", l, r[0])]
                    n = l * (HEADS + KV_HEADS) + i
                    produced(act, j)
                    if i >= 2:
                        act.wait_ge(qk_normed, n - 1)
                    free(nc.scalar.activation(sdb[:, i % 2, :], bank(j)[:, 0:S], ACT.Sqrt, scale=1.0 / HD, bias=eps_c), j)
                elif kind == "v":
                    j = job[("v", l, r[0])]
                    produced(act, j)
                    free(nc.scalar.activation(v_tok[:, r[0], :], bank(j)[:, 0:256], ACT.Copy), j)
                elif kind == "iq":
                    i, j = r[0], job[("iq", l, r[0])]
                    produced(act, j)
                    if i >= 2:
                        act.wait_ge(idx_roped, 5 * l + i - 1)
                    free(nc.scalar.activation(iraw[:, i % 2, :], bank(j)[:, 0:S], ACT.Copy), j)
                elif kind == "idx":
                    t, hd = r
                    j, n, nk = job[("idx", l, t, hd)], (l * TT + t) * IDX_HEADS + hd, P * (t + 1)
                    produced(act, j)
                    if n >= 2:
                        act.wait_ge(idx_summed, n - 1)
                    free(nc.scalar.activation(rel[:, hd % 2, 0:nk], bank(j)[:, 0:nk], ACT.Relu), j)
                elif kind == "a":
                    i, j = r[0], job[("agate", l, r[0])]
                    produced(act, j)
                    if i >= 2:
                        evacuated(act, job[("aval", l, i - 2)])
                    free(nc.scalar.activation(sg[:, i % 2, :], bank(j)[:, 0:S], ACT.Sigmoid), j)
                elif kind in ("cc", "cb"):
                    i, j = r[0], job[(kind, l, r[0])]
                    buf = cct if kind == "cc" else cbt
                    if i >= 2:
                        act.wait_ge(sc_ready, KT * l + i - 1)
                    produced(act, j)
                    free(nc.scalar.activation(buf[:, i % 2, :], bank(j)[:, 0:S], ACT.Copy), j)
                elif kind == "att":
                    n = l * HEADS * TT + r[0] * TT + r[1]
                    nk = P * (r[1] + 1)
                    act.wait_ge(max_ready, n + 1)
                    if n >= 2:
                        act.wait_ge(p_normed, n - 1)
                    do(nc.scalar.activation(pe_[:, n % 2, 0:nk], lg[:, n % 2, 0:nk], ACT.Exp, scale=HD ** -0.5,
                                            bias=stat[:, n % 2:n % 2 + 1], accum_out=stat[:, 2 + n % 2:3 + n % 2]),
                       exp_done, n + 1)
                elif kind == "att_t":
                    hd, t = r
                    j = job[("att_t", l, hd, t)]
                    produced(act, j)
                    free(nc.scalar.activation(pt[:, hd % 2, 0:t + 1, t * P:(t + 1) * P],
                                              bank(j)[:, 0:P * (t + 1)].rearrange("p (k t) -> p k t", k=t + 1),
                                              ACT.Copy), j)
                elif kind == "att_o":
                    j = job[("att_o", l, r[0])]
                    produced(act, j)
                    free(nc.scalar.activation(attn[:, r[0], :], bank(j)[:, 0:S], ACT.Copy), j)
                elif kind == "g":
                    j = job[("g", l, r[0])]
                    produced(act, j)
                    free(nc.scalar.activation(gates[:, r[0], :], bank(j)[:, 0:S], ACT.Sigmoid), j)
                elif kind == "mean":
                    j = job[("mean", l)]
                    produced(act, j)
                    free(nc.scalar.activation(rs[:, 0:S], bank(j)[:, 0:S], ACT.Copy, scale=1.0 / D), j)
                    for k in range(KT):
                        act.wait_ge(centered, KT * l + k + 1)
                        do(nc.scalar.activation(sq1[:, k, :], aconv[:, k, :], ACT.Square), c_squared, KT * l + k + 1)
                elif kind == "var":
                    j = job[("var", l)]
                    produced(act, j)
                    free(nc.scalar.activation(sd[:, 0:S], bank(j)[:, 0:S], ACT.Sqrt, scale=1.0 / D, bias=eps_c), j)
                    for k in range(KT):
                        act.wait_ge(ln_scaled, KT * l + k + 1)
                        do(nc.scalar.activation(aconv[:, k, :], aconv[:, k, :], ACT.Silu, bias=par("ln_b", l, k)),
                           conf_ready, KT * l + k + 1)
                elif kind == "up":
                    i = r[0]
                    n = FT * l + i
                    if n >= 2:
                        act.wait_ge(act_ready, n - 1)
                    for u in range(2):
                        j = job[("up", l, i, u)]
                        ch = u * FT + i
                        produced(act, j)
                        do(nc.scalar.activation(up_buf[:, i % 2, u, :], bank(j)[:, 0:S], ACT.Identity,
                                                scale=par("ffn_w", l, ch * FFN_K + FFN_K - 1), bias=par("ffn_b", l, ch)),
                           up_seeded, 2 * n + u + 1)
                elif kind == "up_act":
                    i = r[0]
                    evacuated(act, job[("up", l, i, 0)])
                    do(nc.scalar.activation(up_buf[:, i % 2, 0, :], up_buf[:, i % 2, 0, :], ACT.Silu), up_silu, FT * l + i + 1)
                elif kind == "mod":
                    i, j = r[0], job[("mod", l, r[0])]
                    produced(act, j)
                    if i >= 2:
                        produced(act, job[("mod_t", l, i - 2)])
                    free(nc.scalar.activation(mod_part[:, i % 2, :], bank(j)[:, 0:256], ACT.Copy), j)
                elif kind == "norm2":
                    n, m = r[0], 3 * l + r[0]
                    T = tokens(l, n)
                    if m == 0:
                        act.wait_ge(context_in, 16)
                    for g in range(KT):
                        before = {0: ("f2", l - 1, 1, g) if l else ("down", DEPTH - 1, g), 1: ("f2", l, 0, g),
                                  2: ("out", l, g)}[n]
                        evacuated(act, job[before])
                        nc.scalar.activation(sq2[:, g, 0:T], x[:, g, 0:T], ACT.Square).then_inc(x2_squared, 1)
                    act.wait_ge(x2_squared, KT * (m + 1))
                    j = job[("ss2", l, n)]
                    produced(act, j)
                    free(nc.scalar.activation(sd[:, 0:T], bank(j)[:, 0:T], ACT.Sqrt, scale=1.0 / D, bias=eps_c), j)
                    for k in range(KT):
                        for s in range(T // S):
                            act.wait_ge(x2_scaled, scaled_count(l, n, k, s))
                            nc.scalar.activation(h[:, k, s * S:(s + 1) * S], h[:, k, s * S:(s + 1) * S], ACT.Identity,
                                                 bias=mod[:, l, 3 * n * KT + k, s:s + 1]).then_inc(h2_ready, 1)
                    act.wait_ge(h2_ready, h2_count(l, n))
                elif kind == "f1":
                    w, i = r
                    T = tokens(l, 2 * w)
                    j = job[("f1", l, w, i)]
                    produced(act, j)
                    if i >= 2:
                        evacuated(act, job[("f3", l, w, i - 2)])
                    free(nc.scalar.activation(silu2[:, i % 2, 0:T], bank(j)[:, 0:T], ACT.Silu), j)
                elif kind == "gate_in":
                    j = job[("gate_in", l)]
                    produced(act, j)
                    free(nc.scalar.activation(g32[0:32, :], bank(j)[0:32, :], ACT.Copy), j)
                elif kind == "gate":
                    d = r[0]
                    j, n = job[("gate", l, d)], 2 * l + d
                    produced(act, j)
                    if n:
                        act.wait_ge(decay_log, n)
                    do(nc.scalar.activation(gabs, bank(j), ACT.Abs, bias=pr2("gate_b" if d else "gate_f", l)), gate_abs, n + 1)
                    do(nc.scalar.activation(gabs, gabs, ACT.Exp, scale=-1.0))
                    do(nc.scalar.activation(gabs, gabs, ACT.Ln, bias=1.0), gate_log, n + 1)
                elif kind == "np":
                    n, i = r
                    j = job[("np", l, n)]
                    T = n_tokens(l, i)
                    produced(act, j)
                    do(nc.scalar.activation(sqb2[:, n % 2, 0:T], bank(j)[:, 0:T], ACT.Square))
                    if n >= 2:
                        act.wait_ge(n_normed, 7 * l + n - 1)
                    free(nc.scalar.activation(raw2[:, n % 2, 0:T], bank(j)[:, 0:T], ACT.Copy), j)
                elif kind == "nss":
                    n, i = r
                    j = job[("nss", l, n)]
                    T = n_tokens(l, i)
                    produced(act, j)
                    if n >= 2:
                        act.wait_ge(n_normed, 7 * l + n - 1)
                    free(nc.scalar.activation(sd2[:, n % 2, 0:T], bank(j)[:, 0:T], ACT.Sqrt, scale=1.0 / HD2, bias=eps_c), j)
                elif kind == "gp":
                    j = job[("gp", l, r[0])]
                    produced(act, j)
                    free(nc.scalar.activation(glaqk[:, r[0], :], bank(j), ACT.Copy, scale=32 ** -0.5 if r[0] == 0 else 1.0), j)
                elif kind == "gv":
                    j = job[("gv", l, r[0])]
                    produced(act, j)
                    free(nc.scalar.activation(glav[:, r[0], :], bank(j)[:, 0:256], ACT.Copy), j)
                elif kind == "rp":
                    j = job[("rp", l, r[0])]
                    produced(act, j)
                    free(nc.scalar.activation(r_t[:, r[0], :], bank(j), ACT.Silu), j)
                elif kind == "vp":
                    j = job[("vp", l, r[0])]
                    produced(act, j)
                    free(nc.scalar.activation(vtok[:, r[0], :], bank(j)[:, 0:384], ACT.Copy), j)
                elif kind == "fp":
                    j = job[("fp", l, r[0])]
                    produced(act, j)
                    free(nc.scalar.activation(four[:, r[0], :], bank(j), ACT.Copy), j)
                elif kind == "g_exp":
                    s = r[0]
                    n = exp_index(l, s)
                    act.wait_ge(exponents, n + 1)
                    lo, hi = (18, 20) if s == 1 and l == DEPTH - 1 else (0, 20) if s == 1 else (0, 18)
                    if s == 1 and l < DEPTH - 1:
                        do(nc.scalar.activation(expo[:, 0:16, :], expo[:, 0:16, :], ACT.Exp, scale=1.0 / TAU))
                        lo = 18
                    do(nc.scalar.activation(expo[:, lo:hi, :], expo[:, lo:hi, :], ACT.Exp, scale=1.0 / TAU), decays, n + 1)
                elif kind == "g_kt":
                    j = job[("g_kt", l)]
                    produced(act, j)
                    free(nc.scalar.activation(k_tok, bank(j).rearrange("p (d t c) -> p d t c", d=2, t=TT), ACT.Copy), j)
                elif kind == "g_s0":
                    j = job[("g_s0", l, r[0])]
                    produced(act, j)
                    free(nc.scalar.activation(s0[:, r[0], :], bank(j)[:, 0:256], ACT.Copy), j)
                elif kind == "four1":
                    j = job[("four1", l, *r)]
                    produced(act, j)
                    free(nc.scalar.activation(fab[:, r[1]], bank(j).rearrange("p (g f c) -> p g f c", g=2, f=2), ACT.Copy), j)
                elif kind == "four2":
                    s, g = r
                    j = job[("four2", l, s, g)]
                    produced(act, j)
                    free(nc.scalar.activation(mixt[:, g, s * S:(s + 1) * S], bank(j)[:, 0:S], ACT.Copy), j)
                elif kind == "g_x":
                    s, hd = r
                    j = job[("g_x", l, s, hd)]
                    produced(act, j)
                    free(nc.scalar.activation(at_m[:, hd, 1:3, :], bank(j)[:, 0:2 * P].rearrange("p (d t) -> p d t", d=2),
                                              ACT.Copy), j)
                elif kind == "g_o":
                    s, pr = r
                    j = job[("g_o", l, s, pr)]
                    produced(act, j)
                    do(nc.scalar.activation(sqb2[:, pr, 0:S], bank(j)[:, 0:S], ACT.Square))
                    free(nc.scalar.activation(raw2[:, pr, 0:S], bank(j)[:, 0:S], ACT.Copy), j)
                elif kind == "g_n":
                    s, pr = r
                    j = job[("g_n", l, s, pr)]
                    produced(act, j)
                    free(nc.scalar.activation(sd2[:, pr, 0:S], bank(j)[:, 0:S], ACT.Sqrt, scale=1.0 / HD2, bias=eps_c), j)
                elif kind == "at":
                    n = at_index(l, r[0])
                    u = mix_units(l == DEPTH - 1)[r[0]]
                    nk = 2 * S if u[1] == 0 else S
                    act.wait_ge(max2_ready, n + 1)
                    if n >= 2:
                        act.wait_ge(p2_normed, n - 1)
                    do(nc.scalar.activation(p2[:, n % 2, 0:nk], bank(job[("at", l, r[0])])[:, 0:nk], ACT.Exp, bias=stat[:, n % 2:n % 2 + 1],
                                            accum_out=stat[:, 2 + n % 2:3 + n % 2]), exp2_done, n + 1)
                elif kind == "at_t":
                    u = mix_units(l == DEPTH - 1)[r[0]]
                    nt = 4 if u[1] == 0 else 2
                    j = job[("at_t", l, r[0])]
                    produced(act, j)
                    free(nc.scalar.activation(pt2[:, (r[0] // 2) % 2, 0:nt, u[3] * P:(u[3] + 1) * P],
                                              bank(j)[:, 0:nt * P].rearrange("p (k t) -> p k t", k=nt), ACT.Copy), j)
                elif kind == "at_o":
                    u = mix_units(l == DEPTH - 1)[r[0]]
                    j = job[("at_o", l, r[0])]
                    produced(act, j)
                    hd = u[2]
                    p0 = 64 * (hd % 2)
                    tile = (2 if u[0] == "na" else 6) + hd // 2
                    free(nc.scalar.activation(mixt[p0:p0 + 64, tile, u[1] * S:(u[1] + 1) * S], bank(j)[p0:p0 + 64, 0:S],
                                              ACT.Copy), j)

        @block.vector
        def _(dve):
            n_step = [0]

            def do(ins, s=None, v=None):
                if s is None:
                    n_step[0] += 1
                    s, v = vector_step, n_step[0]
                ins.then_inc(s, 1)
                dve.wait_ge(s, v)

            def free(ins, j):
                do(ins, bank_free[j % BANKS], freed(j))

            def push(ins):
                n_step[0] += 1
                ins.then_inc(vector_step, 1)

            stt = nc.vector.scalar_tensor_tensor
            tt = nc.vector.tensor_tensor
            ts = nc.vector.tensor_scalar
            do(nc.vector.memset(csil, 0.0))
            do(nc.vector.memset(eps_c, EPS), small_ready, 1)
            dve.wait_ge(x_in, 32)
            dve.wait_ge(inputs_in, 80)
            for l in range(DEPTH):
                for name in ("na_q", "gqa_q"):
                    do(ts(pr2(name, l), pr2(name, l), HD2 ** -0.5, None, ALU.mult))
            for kind, l, *r in steps:
                if kind == "norm":
                    j = job[("ss", l, r[0])]
                    n = 2 * l + r[0]
                    evacuated(dve, j)
                    do(nc.vector.reciprocal(rs[:, 0:S], sd[:, 0:S]))
                    for k in range(KT):
                        stt(h[:, k, 0:S], x[:, k, 0:S], par("norm2" if r[0] else "norm1", l, k), rs[:, 0:S], ALU.mult,
                            ALU.mult).then_inc(h_ready, 1)
                    dve.wait_ge(h_ready, (n + 1) * KT)
                elif kind == "qss":
                    i, j = r[0], job[("qss", l, r[0])]
                    n = l * (HEADS + KV_HEADS) + i
                    evacuated(dve, j)
                    do(nc.vector.reciprocal(tmp, sdb[:, i % 2, :]))
                    if i >= 2:
                        produced(dve, job[("qrot", l, i - 2)])
                    do(stt(qn[:, i % 2, :], raw[:, i % 3, :], par("qg" if i < HEADS else "kg", l), tmp, ALU.mult, ALU.mult),
                       qk_normed, n + 1)
                elif kind == "qrot":
                    i, j = r[0], job[("qrot", l, r[0])]
                    dst = qk_t[:, i, :]
                    do(tt(dst, qn[:, i % 2, :], const("cos_q"), ALU.mult))
                    produced(dve, j)
                    free(tt(tmp, bank(j)[:, 0:S], const("sin_q"), ALU.mult), j)
                    do(tt(dst, dst, tmp, ALU.add), qk_roped, l * (HEADS + KV_HEADS) + i + 1)
                elif kind == "iw":
                    j = job[("iw", l, r[0])]
                    produced(dve, j)
                    free(ts(iw_s[:, r[0], :], bank(j)[:, 0:IDX_HEADS], IDX_HEADS ** -0.5 * IDX_DIM ** -0.5, None, ALU.mult), j)
                elif kind == "irot":
                    i, j = r[0], job[("irot", l, r[0])]
                    dst = iq_t[:, i, :]
                    evacuated(dve, job[("iq", l, i)])
                    do(tt(dst, iraw[:, i % 2, :], const("cos_i"), ALU.mult))
                    produced(dve, j)
                    free(tt(tmp, bank(j)[:, 0:S], const("sin_i"), ALU.mult), j)
                    do(tt(dst, dst, tmp, ALU.add), idx_roped, 5 * l + i + 1)
                elif kind == "idx":
                    t, hd = r
                    j, n, nk = job[("idx", l, t, hd)], (l * TT + t) * IDX_HEADS + hd, P * (t + 1)
                    evacuated(dve, j)
                    w = iw_s[:, t, hd:hd + 1]
                    if hd == 0:
                        ins = ts(score[:, t, 0:nk], rel[:, hd % 2, 0:nk], w, None, ALU.mult)
                    else:
                        ins = stt(score[:, t, 0:nk], rel[:, hd % 2, 0:nk], w, score[:, t, 0:nk], ALU.mult, ALU.add)
                    do(ins, idx_summed, n + 1)
                elif kind == "topk":
                    t = r[0]
                    nk = P * (t + 1)
                    sc, causal = score[:, t, 0:nk], const(f"causal{t}")
                    do(tt(sc, sc, causal, ALU.add))
                    cur, other = sc, work[:, 0:nk]
                    for _ in range(TOP_K // 8):
                        do(nc.vector.max(top8, cur))
                        do(nc.vector.match_replace(other, top8, cur, TAKEN))
                        cur, other = other, cur
                    mb = mbias[:, t, 0:nk]
                    do(ts(mb, cur, TAKEN / 1.5, NEG, ALU.is_gt, ALU.mult))
                    do(tt(mb, mb, causal, ALU.add))
                elif kind == "a":
                    i, j = r[0], job[("aval", l, r[0])]
                    evacuated(dve, job[("agate", l, i)])
                    produced(dve, j)
                    free(tt(aval[:, i, :], bank(j)[:, 0:S], sg[:, i % 2, :], ALU.mult), j)
                elif kind == "conv":
                    i, part = r
                    lo, hi = part * 8, min(part * 8 + 8, CONV_K)
                    for d in range(lo, hi):
                        w = par("conf_w", l, i * CONV_K + CONV_K - 1 - d)
                        if d == 0:
                            do(ts(aconv[:, i, :], aval[:, i, :], w, par("conf_b", l, i), ALU.mult, ALU.add))
                        else:
                            ins = stt(aconv[:, i, d:S], aval[:, i, 0:S - d], w, aconv[:, i, d:S], ALU.mult, ALU.add)
                            if d == CONV_K - 1:
                                do(ins, conv_done, KT * l + i + 1)
                            else:
                                do(ins)
                elif kind == "cx":
                    i = r[0]
                    j = job[("cx", l, i)]
                    evacuated(dve, job[("cc", l, i)])
                    produced(dve, j)
                    free(tt(tmpc, bank(j)[:, 0:S], cct[:, i % 2, :], ALU.mult), j)
                    dst = scv[:, i, :]
                    w = [par("sc_w", l, i * SC_K + SC_K - 1 - d) for d in range(SC_K)]
                    do(ts(dst, tmpc, w[0], None, ALU.mult))
                    for d in (1, 2):
                        do(stt(dst[:, d:S], tmpc[:, 0:S - d], w[d], dst[:, d:S], ALU.mult, ALU.add))
                elif kind == "cb":
                    i, dst = r[0], scv[:, r[0], :]
                    evacuated(dve, job[("cb", l, i)])
                    do(tt(dst, dst, cbt[:, i % 2, :], ALU.mult), sc_ready, KT * l + i + 1)
                elif kind == "att":
                    n = l * HEADS * TT + r[0] * TT + r[1]
                    nk = P * (r[1] + 1)
                    j = job[("att", l, *r)]
                    produced(dve, j)
                    if n >= 2:
                        dve.wait_ge(exp_done, n - 1)
                    free(tt(lg[:, n % 2, 0:nk], bank(j)[:, 0:nk], mbias[:, r[1], 0:nk], ALU.add), j)
                    do(nc.vector.reduce_max(stat[:, 6:7], lg[:, n % 2, 0:nk], AX_X))
                    do(ts(stat[:, n % 2:n % 2 + 1], stat[:, 6:7], -HD ** -0.5, None, ALU.mult), max_ready, n + 1)
                elif kind == "att_n":
                    n = l * HEADS * TT + r[0] * TT + r[1]
                    nk = P * (r[1] + 1)
                    dve.wait_ge(exp_done, n + 1)
                    do(nc.vector.reciprocal(stat[:, 4:5], stat[:, 2 + n % 2:3 + n % 2]))
                    if r[0] * TT + r[1] >= 2:
                        produced(dve, job[("att_t", l, *unit_before(r[0], r[1], 2))])
                    do(ts(pn[:, n % 2, 0:nk], pe_[:, n % 2, 0:nk], stat[:, 4:5], None, ALU.mult), p_normed, n + 1)
                elif kind == "mean":
                    evacuated(dve, job[("mean", l)])
                    for k in range(KT):
                        do(tt(aconv[:, k, :], aconv[:, k, :], rs[:, 0:S], ALU.subtract), centered, KT * l + k + 1)
                elif kind == "var":
                    evacuated(dve, job[("var", l)])
                    do(nc.vector.reciprocal(rs[:, 0:S], sd[:, 0:S]))
                    for k in range(KT):
                        do(stt(aconv[:, k, :], aconv[:, k, :], par("ln_g", l, k), rs[:, 0:S], ALU.mult, ALU.mult),
                           ln_scaled, KT * l + k + 1)
                elif kind == "sc_out":
                    i, j = r[0], job[("sc_out", l, r[0])]
                    evacuated(dve, job[("g", l, 16 + i)])
                    produced(dve, j)
                    free(tt(merged[:, i, :], bank(j)[:, 0:S], gates[:, 16 + i, :], ALU.mult), j)
                elif kind in ("att_out", "conf_out"):
                    i, j = r[0], job[(kind, l, r[0])]
                    g = 8 + i if kind == "att_out" else i
                    evacuated(dve, job[("g", l, g)])
                    produced(dve, j)
                    free(tt(tmpc, bank(j)[:, 0:S], gates[:, g, :], ALU.mult), j)
                    ins = tt(merged[:, i, :], merged[:, i, :], tmpc, ALU.add)
                    if kind == "conf_out":
                        do(ins, merged_ready, KT * l + i + 1)
                    else:
                        do(ins)
                elif kind in ("wo", "down"):
                    i, j = r[0], job[(kind, l, r[0])]
                    produced(dve, j)
                    free(tt(x[:, i, 0:S], bank(j)[:, 0:S], x[:, i, 0:S], ALU.add), j)
                elif kind == "up":
                    i = r[0]
                    for u in range(2):
                        j = job[("up", l, i, u)]
                        ch = u * FT + i
                        dve.wait_ge(up_seeded, 2 * (FT * l + i) + u + 1)
                        for d in (1, 2):
                            o = up_buf[:, i % 2, u, d:S]
                            ins = stt(o, bank(j)[:, 0:S - d], par("ffn_w", l, ch * FFN_K + FFN_K - 1 - d), o, ALU.mult, ALU.add)
                            if d == 1:
                                do(ins)
                            else:
                                free(ins, j)
                elif kind == "up_act":
                    i = r[0]
                    dve.wait_ge(up_silu, FT * l + i + 1)
                    do(tt(act1[:, i, :], up_buf[:, i % 2, 0, :], up_buf[:, i % 2, 1, :], ALU.mult), act_ready, FT * l + i + 1)
                elif kind == "mod_t":
                    i, j = r[0], job[("mod_t", l, r[0])]
                    produced(dve, j)
                    b = par2[:, l * P2_COLS + P2["b_mod"] + 2 * i:l * P2_COLS + P2["b_mod"] + 2 * i + 2]
                    free(tt(mod[:, l, 2 * i:2 * i + 2, :], bank(j)[:, 0:4].rearrange("p (f s) -> p f s", s=2),
                            b.rearrange("p (f s) -> p f s", s=1).to_broadcast([P, 2, 2]), ALU.add), j)
                elif kind == "mod_fin":
                    for n in range(3):
                        m = mod[:, l, (3 * n + 1) * KT:(3 * n + 2) * KT, :]
                        do(ts(m, m, 1.0, None, ALU.add))
                    for n in (2, 8):
                        m = mod[:, l, n * KT:(n + 1) * KT, :]
                        ins = ts(m, m, 0.5, None, ALU.mult)
                        if n == 8:
                            do(ins, mod_ready, l + 1)
                        else:
                            do(ins)
                elif kind == "norm2":
                    n = r[0]
                    T = tokens(l, n)
                    evacuated(dve, job[("ss2", l, n)])
                    do(nc.vector.reciprocal(rs[:, 0:T], sd[:, 0:T]))
                    for k in range(KT):
                        for s in range(T // S):
                            stt(h[:, k, s * S:(s + 1) * S], x[:, k, s * S:(s + 1) * S],
                                mod[:, l, (3 * n + 1) * KT + k, s:s + 1], rs[:, s * S:(s + 1) * S], ALU.mult,
                                ALU.mult).then_inc(x2_scaled, 1)
                    dve.wait_ge(x2_scaled, h2_count(l, n))
                elif kind == "f1":
                    w, i = r
                    T = tokens(l, 2 * w)
                    j = job[("f3", l, w, i)]
                    evacuated(dve, job[("f1", l, w, i)])
                    produced(dve, j)
                    free(tt(act2[:, i, 0:T], bank(j)[:, 0:T], silu2[:, i % 2, 0:T], ALU.mult), j)
                elif kind in ("f2", "out"):
                    i = r[-1]
                    n = {"out": 5}.get(kind) or (2 if r[0] == 0 else 8)
                    T = 2 * S if n == 2 or l < DEPTH - 1 else S
                    j = job[(kind, l, *r)]
                    produced(dve, j)
                    for s in range(T // S):
                        xs = x[:, i, s * S:(s + 1) * S]
                        ins = stt(xs, bank(j)[:, s * S:(s + 1) * S], mod[:, l, n * KT + i, s:s + 1], xs, ALU.mult, ALU.add)
                        if s == T // S - 1:
                            free(ins, j)
                        else:
                            do(ins)
                elif kind == "gate":
                    d = r[0]
                    j, n = job[("gate", l, d)], 2 * l + d
                    dve.wait_ge(gate_abs, n + 1)
                    free(ts(la[:, d, :], bank(j), pr2("gate_b" if d else "gate_f", l), 0.0, ALU.add, ALU.min), j)
                    dve.wait_ge(gate_log, n + 1)
                    do(tt(la[:, d, :], la[:, d, :], gabs, ALU.subtract), decay_log, n + 1)
                elif kind == "nss":
                    n, i = r
                    j = job[("nss", l, n)]
                    T = n_tokens(l, i)
                    gain = {0: "na_q", 1: "na_q", 2: "na_k", 3: "na_k", 4: "gqa_q", 5: "gqa_q", 6: "gqa_k"}[i]
                    evacuated(dve, j)
                    do(nc.vector.reciprocal(tmp2[:, 0:T], sd2[:, n % 2, 0:T]))
                    do(stt(nq[:, i, 0:T], raw2[:, n % 2, 0:T], pr2(gain, l), tmp2[:, 0:T], ALU.mult, ALU.mult),
                       n_normed, 7 * l + n + 1)
                elif kind == "nrot":
                    n, i = r
                    j = job[("nrot", l, n)]
                    produced(dve, j)
                    free(tt(tmp2[:, 0:S], bank(j)[:, 0:S], const("sin_g"), ALU.mult), j)
                    do(tt(nq[:, i, 0:S], nq[:, i, 0:S], const("cos_g"), ALU.mult))
                    do(tt(nq[:, i, 0:S], nq[:, i, 0:S], tmp2[:, 0:S], ALU.add), n_roped, 3 * l + n + 1)
                elif kind == "g_exp":
                    s = r[0]
                    n = exp_index(l, s)
                    one = ones[:, 0:1].to_broadcast([P, S])
                    if n:
                        produced(dve, job[("g_s0", l, 1)] if s == 0 else job[("g_o", l - 1, 0, 1)])
                        if s == 0 and l < DEPTH - 1:
                            produced(dve, job[("g_lv", l, 1, 3, GLA_LEVELS // 2 - 1)])
                    do(nc.vector.tensor_tensor_scan(cum_f, one, la[:, 0, s * S:(s + 1) * S], 0.0, ALU.mult, ALU.add))
                    do(nc.vector.memset(cum_b[:, 0:1], 0.0))
                    do(nc.vector.tensor_tensor_scan(cum_b[:, 1:S + 1], one, la[:, 1, s * S:(s + 1) * S], 0.0, ALU.mult, ALU.add))
                    ex = cum_b[:, 0:S]
                    if not (s == 1 and l == DEPTH - 1):
                        for lv in range(GLA_LEVELS):
                            m = P >> lv
                            nb = S // (2 * m)
                            f3 = cum_f.rearrange("p (b t) -> p b t", t=2 * m)
                            b3 = ex.rearrange("p (b t) -> p b t", t=2 * m)
                            q3 = expo[:, lv, :].rearrange("p (b t) -> p b t", t=2 * m)
                            k3 = expo[:, 8 + lv, :].rearrange("p (b t) -> p b t", t=2 * m)
                            mid_f = f3[:, :, m - 1:m].to_broadcast([P, nb, m])
                            mid_b = b3[:, :, m:m + 1].to_broadcast([P, nb, m])
                            push(tt(q3[:, :, m:2 * m], f3[:, :, m:2 * m], mid_f, ALU.subtract))
                            push(tt(k3[:, :, 0:m], mid_f, f3[:, :, 0:m], ALU.subtract))
                            push(tt(q3[:, :, 0:m], mid_b, b3[:, :, 0:m], ALU.subtract))
                            push(tt(k3[:, :, m:2 * m], b3[:, :, m:2 * m], mid_b, ALU.subtract))
                        dve.wait_ge(vector_step, n_step[0])
                    if s == 0:
                        do(nc.vector.tensor_copy(expo[:, 16, :], cum_f))
                        do(tt(expo[:, 17, :], cum_b[:, S:S + 1].to_broadcast([P, S]), ex, ALU.subtract), exponents, n + 1)
                    else:
                        do(tt(expo[:, 18, :], cum_f[:, S - 1:S].to_broadcast([P, S]), cum_f, ALU.subtract))
                        do(nc.vector.tensor_copy(expo[:, 19, :], ex), exponents, n + 1)
                    if not (s == 1 and l == DEPTH - 1):
                        dve.wait_ge(decays, n + 1)
                        kk = glaqk[:, 1:2, s * S:(s + 1) * S].to_broadcast([P, 8, S])
                        do(tt(expo[:, 8:16, :], expo[:, 8:16, :], kk, ALU.mult), k_decayed, kdec(l, s))
                elif kind == "g_lv":
                    s, hd, lp = r
                    j = job[("g_lv", l, s, hd, lp)]
                    mask = const("level").rearrange("p (v a c) -> p v a c", v=GLA_LEVELS, a=1)[:, 2 * lp:2 * lp + 2]
                    mask = mask.to_broadcast([P, 2, TT, P])
                    four_blocks = lambda v: v.rearrange("p v (t c) -> p v t c", t=TT)
                    src = bank(j).rearrange("p (v t c) -> p v t c", v=2, t=TT)
                    produced(dve, j)
                    if lp == 0:
                        free(tt(four_blocks(gacc), src, mask, ALU.mult), j)
                    else:
                        free(tt(four_blocks(gtmp), src, mask, ALU.mult), j)
                        do(tt(gacc, gacc, gtmp, ALU.add))
                    if lp == GLA_LEVELS // 2 - 1:
                        g3 = four_blocks(gacc)
                        do(tt(at_m[:, hd, 0:4:3, :], g3[:, 0], g3[:, 1], ALU.add), level_added, lev(l, s, hd))
                elif kind == "g_n":
                    s, pr = r
                    n = gla_index(l, s, pr)
                    evacuated(dve, job[("g_n", l, s, pr)])
                    do(nc.vector.reciprocal(tmp2[:, 0:S], sd2[:, pr, 0:S]))
                    do(stt(raw2[:, pr, 0:S], raw2[:, pr, 0:S], pr2("gla_n", l), tmp2[:, 0:S], ALU.mult, ALU.mult))
                    do(tt(mixt[:, 4 + pr, s * S:(s + 1) * S], raw2[:, pr, 0:S], r_t[:, pr, s * S:(s + 1) * S], ALU.mult),
                       gla_ready, n + 1)
                elif kind == "na_bias":
                    at, _n = CONST["window"]
                    win = consts[:, at:at + TT * S].rearrange("p (t k) -> p t k", t=TT)
                    for hd in range(4):
                        j = job[("flip", l, hd)]
                        produced(dve, j)
                        free(tt(nab[:, hd], bank(j).rearrange("p (t k) -> p t k", t=TT), win, ALU.add), j)
                elif kind == "at":
                    n = at_index(l, r[0])
                    u = mix_units(l == DEPTH - 1)[r[0]]
                    nk = 2 * S if u[1] == 0 else S
                    j = job[("at", l, r[0])]
                    produced(dve, j)
                    if n >= 2:
                        dve.wait_ge(exp2_done, n - 1)
                    do(nc.vector.reduce_max(stat[:, 6:7], bank(j)[:, 0:nk], AX_X))
                    do(ts(stat[:, n % 2:n % 2 + 1], stat[:, 6:7], -1.0, None, ALU.mult), max2_ready, n + 1)
                elif kind == "at_n":
                    n = at_index(l, r[0])
                    u = mix_units(l == DEPTH - 1)[r[0]]
                    nk = 2 * S if u[1] == 0 else S
                    dve.wait_ge(exp2_done, n + 1)
                    free(nc.vector.reciprocal(stat[:, 4:5], stat[:, 2 + n % 2:3 + n % 2]), job[("at", l, r[0])])
                    if r[0] >= 2:
                        produced(dve, job[("at_t", l, r[0] - 2)])
                    do(ts(pn2[:, n % 2, 0:nk], p2[:, n % 2, 0:nk], stat[:, 4:5], None, ALU.mult), p2_normed, n + 1)

        @block.tensor
        def _(pe):
            mm = nc.tensor.matmul

            def begin(j):
                if j >= BANKS:
                    pe.wait_ge(bank_free[j % BANKS], j // BANKS)
                return bank(j)

            def arrived(name):
                pe.wait_ge(loaded[slot_of[name]], ready_at[name])
                return weights(name)

            def done(ins):
                ins.then_inc(product_done, 1)

            def project(j, w, c0, src, T, rows_=P, ready=None):
                o = begin(j)
                kt = w.shape[1]
                for k in range(kt):
                    if ready:
                        pe.wait_ge(ready[0], ready[1] + ready[2] * (k + 1))
                    ins = mm(o[0:rows_, 0:T], w[:, k, c0:c0 + rows_], src[:, k, 0:T], start=(k == 0), stop=(k == kt - 1))
                done(ins)

            def project_tok(j, w, c0, n, t):
                o = begin(j)
                for k in range(KT):
                    ins = mm(o[:, 0:n], h[:, k, t * P:(t + 1) * P], w[:, k, c0:c0 + n], start=(k == 0), stop=(k == KT - 1))
                done(ins)

            pe.wait_ge(x_in, 32)
            for kind, l, *r in steps:
                if kind == "norm":
                    n = 2 * l + r[0]
                    o = begin(job[("ss", l, r[0])])
                    for k in range(KT):
                        pe.wait_ge(x_squared, n * KT + k + 1)
                        ins = mm(o[:, 0:S], ones, sq1[:, k, :], start=(k == 0), stop=(k == KT - 1))
                    done(ins)
                elif kind == "qk":
                    i = r[0]
                    if (l, i) == (0, 0):
                        pe.wait_ge(inputs_in, 80)
                        pe.wait_ge(c_ready, 1)
                    project(job[("qk", l, i)], arrived(("qk", l, i // 2)), P * (i % 2), h, S,
                            ready=(h_ready, 2 * l * KT, 1) if i == 0 else None)
                elif kind == "qss":
                    i, j = r[0], job[("qss", l, r[0])]
                    evacuated(pe, job[("qk", l, i)])
                    done(mm(begin(j)[:, 0:S], ones, sqb[:, i % 2, :], start=True, stop=True))
                elif kind == "qrot":
                    i, j = r[0], job[("qrot", l, r[0])]
                    pe.wait_ge(qk_normed, l * (HEADS + KV_HEADS) + i + 1)
                    done(mm(begin(j)[:, 0:S], const("rot_q"), qn[:, i % 2, :], start=True, stop=True))
                elif kind == "v":
                    project_tok(job[("v", l, r[0])], arrived(("v", l)), 0, 256, r[0])
                elif kind == "iq":
                    i = r[0]
                    project(job[("iq", l, i)], arrived(("iq", l, i // 2)), P * (i % 2), h, S)
                elif kind == "iw":
                    project_tok(job[("iw", l, r[0])], arrived(("iq", l, 2)), P, IDX_HEADS, r[0])
                elif kind == "irot":
                    i, j = r[0], job[("irot", l, r[0])]
                    evacuated(pe, job[("iq", l, i)])
                    done(mm(begin(j)[:, 0:S], const("rot_i"), iraw[:, i % 2, :], start=True, stop=True))
                elif kind == "idx":
                    t, hd = r
                    nk = P * (t + 1)
                    p0 = 64 * (hd % 2)
                    pe.wait_ge(idx_roped, 5 * l + 5)
                    done(mm(begin(job[("idx", l, t, hd)])[:, 0:nk], iq_t[p0:p0 + 64, hd // 2, t * P:(t + 1) * P],
                            iq_t[p0:p0 + 64, 4, 0:nk], start=True, stop=True))
                elif kind == "a":
                    w = arrived(("a", l, r[0]))
                    project(job[("agate", l, r[0])], w, 0, h, S)
                    project(job[("aval", l, r[0])], w, P, h, S)
                elif kind in ("cc", "cx", "cb"):
                    project(job[(kind, l, r[0])], arrived(("c", l, r[0])), P * ("cc", "cx", "cb").index(kind), h, S)
                elif kind == "g":
                    project(job[("g", l, r[0])], arrived(("g", l, r[0] // 2)), P * (r[0] % 2), h, S)
                elif kind == "att":
                    hd, t = r
                    nk = P * (t + 1)
                    pe.wait_ge(qk_roped, (l + 1) * (HEADS + KV_HEADS))
                    done(mm(begin(job[("att", l, hd, t)])[:, 0:nk], qk_t[:, hd, t * P:(t + 1) * P],
                            qk_t[:, HEADS + hd // (HEADS // KV_HEADS), 0:nk], start=True, stop=True))
                elif kind == "att_t":
                    hd, t = r
                    n = l * HEADS * TT + hd * TT + t
                    pe.wait_ge(p_normed, n + 1)
                    o = begin(job[("att_t", l, hd, t)])
                    for k in range(t + 1):
                        ins = nc.tensor.transpose(o[:, k * P:(k + 1) * P], pn[:, n % 2, k * P:(k + 1) * P], ident)
                    done(ins)
                elif kind == "att_o":
                    hd = r[0]
                    g = hd // (HEADS // KV_HEADS)
                    for t in range(TT):
                        evacuated(pe, job[("att_t", l, hd, t)])
                    o = begin(job[("att_o", l, hd)])
                    mm(o[:, 0:S], v_tok[:, 0, g * HD:(g + 1) * HD], pt[:, hd % 2, 0, :], start=True, stop=False)
                    done(mm(o[:, P:S], v_tok[:, 1, g * HD:(g + 1) * HD], pt[:, hd % 2, 1, P:S], start=False, stop=True))
                elif kind == "mean":
                    o = begin(job[("mean", l)])
                    for k in range(KT):
                        pe.wait_ge(conv_done, KT * l + k + 1)
                        ins = mm(o[:, 0:S], ones, aconv[:, k, :], start=(k == 0), stop=(k == KT - 1))
                    done(ins)
                elif kind == "var":
                    o = begin(job[("var", l)])
                    for k in range(KT):
                        pe.wait_ge(c_squared, KT * l + k + 1)
                        ins = mm(o[:, 0:S], ones, sq1[:, k, :], start=(k == 0), stop=(k == KT - 1))
                    done(ins)
                elif kind in ("sc_out", "att_out", "conf_out", "wo"):
                    i = r[0]
                    if kind == "sc_out":
                        pe.wait_ge(sc_ready, KT * (l + 1))
                    elif kind == "att_out":
                        evacuated(pe, job[("att_o", l, HEADS - 1)])
                    elif kind == "conf_out":
                        pe.wait_ge(conf_ready, KT * (l + 1))
                    else:
                        pe.wait_ge(merged_ready, KT * (l + 1))
                    src = {"sc_out": scv, "att_out": attn, "conf_out": aconv, "wo": merged}[kind]
                    project(job[(kind, l, i)], arrived((kind, l, i // 2)), P * (i % 2), src, S)
                elif kind == "up":
                    w = arrived(("up", l, r[0]))
                    for u in range(2):
                        project(job[("up", l, r[0], u)], w, P * u, h, S,
                                ready=(h_ready, (2 * l + 1) * KT, 1) if r[0] == u == 0 else None)
                elif kind == "down":
                    pe.wait_ge(act_ready, FT * (l + 1))
                    project(job[("down", l, r[0])], arrived(("down", l, r[0])), 0, act1, S)
                elif kind == "mod":
                    i, j = r[0], job[("mod", l, r[0])]
                    w = arrived(("mod", l, i))
                    o = begin(j)
                    for k in range(KT):
                        g = k % 4
                        ins = mm(o[32 * g:32 * g + 32, 0:256], csil[:, k, :], w[:, k, :], start=(k < 4), stop=(k >= 4))
                    done(ins)
                elif kind == "mod_t":
                    i, j = r[0], job[("mod_t", l, r[0])]
                    evacuated(pe, job[("mod", l, i)])
                    o = begin(j)
                    for f in range(2):
                        ins = mm(o[:, 2 * f:2 * f + 2], mod_part[:, i % 2, f * P:(f + 1) * P], const("sel"),
                                 start=True, stop=True)
                    done(ins)
                elif kind == "norm2":
                    n = r[0]
                    T = tokens(l, n)
                    o = begin(job[("ss2", l, n)])
                    for k in range(KT):
                        pe.wait_ge(x2_squared, KT * (3 * l + n) + k + 1)
                        ins = mm(o[:, 0:T], ones, sq2[:, k, 0:T], start=(k == 0), stop=(k == KT - 1))
                    done(ins)
                elif kind == "f1":
                    w, i = r
                    wt = arrived(("f1", l, w, i))
                    project(job[("f1", l, w, i)], wt, 0, h, tokens(l, 2 * w),
                            ready=h2_tiles(l, 2 * w) if i == 0 else None)
                    project(job[("f3", l, w, i)], wt, P, h, tokens(l, 2 * w))
                elif kind == "f2":
                    w, i = r
                    if i == 0:
                        evacuated(pe, job[("f3", l, w, FT - 1)])
                    project(job[("f2", l, w, i)], arrived(("f2", l, w, i)), 0, act2, tokens(l, 2 * w))
                elif kind == "gate_in":
                    project(job[("gate_in", l)], arrived(("w2", l, "gk")), P, h, 2 * S, 32,
                            ready=h2_tiles(l, 1))
                elif kind == "gate":
                    d = r[0]
                    evacuated(pe, job[("gate_in", l)])
                    done(mm(begin(job[("gate", l, d)]), gw[0:32, l, d, :], g32[0:32, :], start=True, stop=True))
                elif kind == "np":
                    n, i = r
                    name = {6: "gk", 4: "gq", 5: "gq", 0: "naq", 1: "naq", 2: "nak", 3: "nak"}[i]
                    w = arrived(("w2", l, name))
                    T = n_tokens(l, i)
                    project(job[("np", l, n)], w, P * (i % 2) if i < 6 else 0, h, T)
                elif kind == "nss":
                    n, i = r
                    T = n_tokens(l, i)
                    evacuated(pe, job[("np", l, n)])
                    done(mm(begin(job[("nss", l, n)])[:, 0:T], ones64, sqb2[:, n % 2, 0:T], start=True, stop=True))
                elif kind == "nrot":
                    n, i = r
                    pe.wait_ge(n_normed, 7 * l + n + 1)
                    done(mm(begin(job[("nrot", l, n)])[:, 0:S], const("rot_g"), nq[:, i, 0:S], start=True, stop=True))
                elif kind == "gp":
                    project(job[("gp", l, r[0])], arrived(("w2", l, "glaqk")), P * r[0], h, 2 * S)
                elif kind == "gv":
                    project_tok(job[("gv", l, r[0])], arrived(("w2", l, "glav")), 0, 256, r[0])
                elif kind == "rp":
                    project(job[("rp", l, r[0])], arrived(("w2", l, "glar")), P * r[0], h, 2 * S)
                elif kind == "vp":
                    project_tok(job[("vp", l, r[0])], arrived(("w2", l, "v")), 0, 384, r[0])
                elif kind == "fp":
                    project(job[("fp", l, r[0])], arrived(("w2", l, "four")), P * r[0], h, 2 * S)
                elif kind == "g_kt":
                    pe.wait_ge(q_decayed, exp_index(l, 1) + 1)
                    o = begin(job[("g_kt", l)])
                    for d in range(2):
                        for t in range(TT):
                            c0 = (d * TT + t) * P
                            ins = nc.tensor.transpose(o[:, c0:c0 + P], expo[:, 18 + d, t * P:(t + 1) * P], ident)
                    done(ins)
                elif kind == "g_s0":
                    d = r[0]
                    evacuated(pe, job[("g_kt", l)])
                    evacuated(pe, job[("gv", l, 2 * TT - 1)])
                    o = begin(job[("g_s0", l, d)])
                    for t in range(TT):
                        ins = mm(o[:, 0:256], k_tok[:, d, t, :], glav[:, TT + t, :], start=(t == 0), stop=(t == TT - 1))
                    done(ins)
                elif kind == "g_x":
                    s, hd = r
                    pe.wait_ge(q_decayed, exp_index(l, s) + 1)
                    pe.wait_ge(k_decayed, kdec(l, s))
                    o = begin(job[("g_x", l, s, hd)])
                    ph = slice(32 * hd, 32 * hd + 32)
                    for d in range(2):
                        ins = mm(o[:, d * P:(d + 1) * P], expo[ph, 8, d * P:(d + 1) * P], expo[ph, 0, (1 - d) * P:(2 - d) * P],
                                 start=True, stop=True)
                    done(ins)
                elif kind == "g_lv":
                    s, hd, lp = r
                    o = begin(job[("g_lv", l, s, hd, lp)])
                    ph = slice(32 * hd, 32 * hd + 32)
                    for v in range(2):
                        lv = 2 * lp + v + 1
                        for t in range(TT):
                            if lv < GLA_LEVELS:
                                kq = expo[ph, 8 + lv, t * P:(t + 1) * P], expo[ph, lv, t * P:(t + 1) * P]
                            else:
                                cols = slice(s * S + t * P, s * S + (t + 1) * P)
                                kq = glaqk[ph, 1, cols], glaqk[ph, 0, cols]
                            c0 = (v * TT + t) * P
                            ins = mm(o[:, c0:c0 + P], *kq, start=True, stop=True)
                    done(ins)
                elif kind == "g_o":
                    s, pr = r
                    evacuated(pe, job[("g_x", l, s, 2 * pr + 1)])
                    pe.wait_ge(level_added, lev(l, s, 2 * pr + 1))
                    if s == 0:
                        evacuated(pe, job[("g_s0", l, 1)])
                    o = begin(job[("g_o", l, s, pr)])
                    for hh_ in range(2):
                        hd = 2 * pr + hh_
                        oo = o[64 * hh_:64 * hh_ + 64, 0:S]
                        ec = slice(hd * HD2, (hd + 1) * HD2)
                        ph = slice(32 * hd, 32 * hd + 32)
                        for t in range(TT):
                            ins = mm(oo, glav[:, s * TT + t, ec], at_m[:, hd, 2 * t:2 * t + 2, :], start=(t == 0),
                                     stop=(s == 1 and t == TT - 1))
                        if s == 0:
                            for d in range(2):
                                ins = mm(oo, s0[ph, d, ec], expo[ph, 16 + d, :], start=False, stop=(d == 1))
                    done(ins)
                elif kind == "g_n":
                    s, pr = r
                    evacuated(pe, job[("g_o", l, s, pr)])
                    done(mm(begin(job[("g_n", l, s, pr)])[:, 0:S], ones64, sqb2[:, pr, 0:S], start=True, stop=True))
                elif kind == "four1":
                    s, t = r
                    evacuated(pe, job[("fp", l, 1)])
                    o = begin(job[("four1", l, s, t)])
                    for g in range(2):
                        ins = mm(o[:, g * 256:(g + 1) * 256], four[:, g, s * S + t * P:s * S + (t + 1) * P], const("dft_d"),
                                 start=True, stop=True)
                    done(ins)
                elif kind == "four2":
                    s, g = r
                    for t in range(TT):
                        evacuated(pe, job[("four1", l, s, t)])
                    o = begin(job[("four2", l, s, g)])
                    for t in range(TT):
                        for f, name in enumerate(("cos_l", "sin_l")):
                            ins = mm(o[:, 0:S], fab[:, t, g, f, :], const(name)[:, t * S:(t + 1) * S],
                                     start=(t == 0 and f == 0), stop=(t == TT - 1 and f == 1))
                    done(ins)
                elif kind == "at":
                    kk, s, hd, t = mix_units(l == DEPTH - 1)[r[0]]
                    pe.wait_ge(n_roped, 3 * l + 3)
                    pe.wait_ge(n_normed, 7 * l + 7)
                    if kk == "na":
                        p0 = 64 * (hd % 2)
                        qi, ki = hd // 2, 2 + hd // 2
                    else:
                        p0 = 64 * (hd // 2)
                        qi, ki = 4 + hd % 2, 6
                    c0, nk = (0, 2 * S) if s == 0 else (S, S)
                    o = begin(job[("at", l, r[0])])
                    biased = kk == "na" and s == 0
                    ins = mm(o[:, 0:nk], nq[p0:p0 + 64, qi, s * S + t * P:s * S + (t + 1) * P],
                             nq[p0:p0 + 64, ki, c0:c0 + nk], start=True, stop=not biased)
                    if biased:
                        if (hd, t) == (0, 0):
                            evacuated(pe, job[("flip", l, 3)])
                        ins = mm(o[:, 0:S], ident, nab[:, hd, t, :], start=False, stop=True)
                    done(ins)
                elif kind == "at_t":
                    n = at_index(l, r[0])
                    u = mix_units(l == DEPTH - 1)[r[0]]
                    nt = 4 if u[1] == 0 else 2
                    pe.wait_ge(p2_normed, n + 1)
                    o = begin(job[("at_t", l, r[0])])
                    for k in range(nt):
                        ins = nc.tensor.transpose(o[:, k * P:(k + 1) * P], pn2[:, n % 2, k * P:(k + 1) * P], ident)
                    done(ins)
                elif kind == "at_o":
                    kk, s, hd, t = mix_units(l == DEPTH - 1)[r[0]]
                    for d in range(TT):
                        evacuated(pe, job[("at_t", l, r[0] + d)])
                    p0 = 64 * (hd % 2)
                    vc = hd * HD2 if kk == "na" else 256 + (hd // 2) * HD2
                    tiles = [0, 1, 2, 3] if s == 0 else [2, 3]
                    o = begin(job[("at_o", l, r[0])])
                    for n, kt in enumerate(tiles):
                        ins = mm(o[p0:p0 + 64, 0:S], vtok[:, kt, vc:vc + HD2], pt2[:, (r[0] // 2) % 2, n, :],
                                 start=(n == 0), stop=(n == len(tiles) - 1))
                    done(ins)
                elif kind == "na_bias":
                    pe.wait_ge(bias_in, 256 * (l + 1))
                    for hd in range(4):
                        done(mm(begin(job[("flip", l, hd)]), const("flip"), nab_raw[:, hd], start=True, stop=True))
                elif kind == "out":
                    i = r[0]
                    if i == 0:
                        n = len(mix_units(l == DEPTH - 1))
                        evacuated(pe, job[("at_o", l, n - 2)])
                        pe.wait_ge(gla_ready, gla_count(l, True))
                    project(job[("out", l, i)], arrived(("out", l, i // 2)), P * (i % 2), mixt,
                            2 * S if l < DEPTH - 1 else S)


INPUTS = ["w_in", "w_attn_out", "w_conf_out", "w_sc_out", "w_o", "w_up", "w_down", "w_mod_2", "ffn1_w1_2", "ffn1_w3_2",
          "ffn1_w2_2", "w_in_2", "na_rpb_2", "w_out_2", "ffn2_w1_2", "ffn2_w3_2", "ffn2_w2_2"]


def columns(v, width=P):
    v = np.asarray(v)
    v = v.reshape(v.shape[0], -1, v.shape[-1] // width, width)
    return v.transpose(0, 3, 2, 1).reshape(v.shape[0], width, -1)


def lay_out(inputs):
    i = {k: np.asarray(v) for k, v in inputs.items()}
    arrays = {n: np.ascontiguousarray(i[n]) for n in INPUTS}
    arrays["x"] = np.ascontiguousarray(i["x"][0].T)
    arrays["ctx"] = np.ascontiguousarray(i["ctx_2"][0].T)
    arrays["c2"] = np.ascontiguousarray(np.stack([i["c_2"][0], i["c_ctx_2"]], axis=1))
    arrays["par1"] = np.ascontiguousarray(np.concatenate(
        [columns(i[n]) for n in ("norm1_g", "norm2_g", "q_norm_g", "k_norm_g", "conf_conv_w", "conf_conv_b", "conf_ln_g",
                                 "conf_ln_b", "sc_conv_w", "ffn_conv_w", "ffn_conv_b")], axis=2))
    twice = lambda n: np.concatenate([i[n], i[n]], axis=1)
    arrays["par2"] = np.ascontiguousarray(np.concatenate(
        [columns(v) for v in (i["b_mod_2"], twice("na_q_norm_2"), twice("na_k_norm_2"), twice("gla_norm_2"),
                              twice("gqa_q_norm_2"), twice("gqa_k_norm_2"), i["gla_b_gate_f_2"], i["gla_b_gate_b_2"])],
        axis=2))
    zero = np.zeros_like(i["gla_w_gate_f_2"])
    arrays["gate_w"] = np.ascontiguousarray(np.stack(
        [np.concatenate([i["gla_w_gate_f_2"], zero], axis=1), np.concatenate([zero, i["gla_w_gate_b_2"]], axis=1)], axis=1))
    arrays["consts"] = shape_constants()
    return arrays


def kernel(**inputs):
    import concourse.bacc as bacc
    from concourse.bass_utils import run_bass_kernel_spmd

    nc = bacc.Bacc("TRN2", target_bir_lowering=False, num_devices=1)
    arrays = lay_out(inputs)
    handles = {n: nc.dram_tensor(f"in_{n}", v.shape, F32, kind="ExternalInput").ap() for n, v in arrays.items()}
    out = nc.dram_tensor("out_x", (D, S), F32, kind="ExternalOutput").ap()
    build(nc, handles, out)
    result = run_bass_kernel_spmd(nc, [{f"in_{n}": v for n, v in arrays.items()}], core_ids=[0])
    return np.ascontiguousarray(result.results[0]["out_x"].T)[None]
```
